# Optimizing a Trainium2 kernel written in Bass

```python
import math
import jax, jax.numpy as jnp
from jax import lax
import numpy as np

D_MODEL = 1024
BATCH = 1
SEQ = 256
DEPTH = 2

N_MIXERS = 2
N_RET_LAYERS = (DEPTH + N_MIXERS - 1) // N_MIXERS
N_SB_LAYERS = DEPTH // N_MIXERS
PLE_DIM = 256
D_FF = 2816
FFN_RES_WEIGHT = 0.5
RET_HEADS = 4
RET_DK = D_MODEL // RET_HEADS
RET_QK = RET_HEADS * RET_DK
RET_DV = 2 * RET_DK
RET_V = RET_HEADS * RET_DV
RET_IN = 2 * RET_QK + 2 * RET_V
RET_CHUNK = 128
ROPE_BASE = 10000.0
GN_EPS = 1e-5
SB_HEADS = 8
SB_DH = D_MODEL // SB_HEADS
SB_WIDTH = SB_HEADS * SB_DH
SB_IN = 3 * SB_WIDTH
SB_BLOCK = 128
N_NORMS = 8
RMS_EPS = 1e-6


def rmsnorm(x, g):
    xf = x.astype(jnp.float32)
    y = xf * lax.rsqrt(jnp.mean(xf * xf, axis=-1, keepdims=True) + RMS_EPS)
    return (y * g.astype(jnp.float32)).astype(x.dtype)

def swiglu(x, w_gate, w_up, w_down):
    return (jax.nn.silu(x @ w_gate) * (x @ w_up)) @ w_down

def rope(t, positions):
    half = t.shape[-1] // 2
    inv = ROPE_BASE ** (-jnp.arange(half, dtype=jnp.float32) / half)
    ang = positions.astype(jnp.float32)[..., None] * inv
    cos = jnp.cos(ang)[:, :, None, :]
    sin = jnp.sin(ang)[:, :, None, :]
    t1, t2 = t[..., :half], t[..., half:]
    return jnp.concatenate([t1 * cos - t2 * sin, t1 * sin + t2 * cos], axis=-1)

def retention(h, positions, w_in, gn_gain, w_out):
    B, S, _ = h.shape
    proj = h @ w_in
    q, k, v, g = jnp.split(proj, [RET_QK, 2 * RET_QK, 2 * RET_QK + RET_V], axis=-1)
    q = rope(q.astype(jnp.float32).reshape(B, S, RET_HEADS, RET_DK), positions)
    k = rope(k.astype(jnp.float32).reshape(B, S, RET_HEADS, RET_DK), positions) * (RET_DK ** -0.5)
    v = v.astype(jnp.float32).reshape(B, S, RET_HEADS, RET_DV)

    nc = S // RET_CHUNK
    def to_chunks(t):
        return t.reshape(B, nc, RET_CHUNK, RET_HEADS, -1).transpose(1, 0, 3, 2, 4)
    qc, kc, vc = to_chunks(q), to_chunks(k), to_chunks(v)

    log_gamma = jnp.log1p(-jnp.exp2(-5.0 - jnp.arange(RET_HEADS, dtype=jnp.float32)))
    idx = jnp.arange(RET_CHUNK, dtype=jnp.float32)
    rel = idx[:, None] - idx[None, :]
    inner_decay = jnp.where(rel[None] >= 0,
                            jnp.exp(jnp.maximum(rel, 0.0)[None] * log_gamma[:, None, None]),
                            0.0)
    xi = jnp.exp((idx + 1.0)[None, :] * log_gamma[:, None])
    zeta = jnp.exp((RET_CHUNK - 1.0 - idx)[None, :] * log_gamma[:, None])
    chunk_decay = jnp.exp(RET_CHUNK * log_gamma)

    def step(state, inp):
        qi, ki, vi = inp
        scores = jnp.einsum('bhid,bhjd->bhij', qi, ki) * inner_decay[None]
        o_inner = jnp.einsum('bhij,bhjv->bhiv', scores, vi)
        o_cross = jnp.einsum('bhid,bhdv->bhiv', qi, state) * xi[None, :, :, None]
        new_state = state * chunk_decay[None, :, None, None] + jnp.einsum(
            'bhjd,bhjv->bhdv', ki * zeta[None, :, :, None], vi)
        return new_state, o_inner + o_cross

    state0 = jnp.zeros((B, RET_HEADS, RET_DK, RET_DV), jnp.float32)
    _, o = lax.scan(step, state0, (qc, kc, vc))
    o = o.transpose(1, 0, 3, 2, 4).reshape(B, S, RET_HEADS, RET_DV)
    mu = jnp.mean(o, axis=-1, keepdims=True)
    var = jnp.mean(jnp.square(o - mu), axis=-1, keepdims=True)
    o = ((o - mu) * lax.rsqrt(var + GN_EPS)).reshape(B, S, RET_V) * gn_gain.astype(jnp.float32)
    o = jax.nn.silu(g.astype(jnp.float32)) * o
    return o.astype(h.dtype) @ w_out

def stick_breaking(h, w_in, w_out):
    B, S, _ = h.shape
    proj = h @ w_in
    q, k, v = jnp.split(proj, [SB_WIDTH, 2 * SB_WIDTH], axis=-1)
    def heads(t):
        return t.astype(jnp.float32).reshape(B, S, SB_HEADS, SB_DH).transpose(0, 2, 1, 3)
    q, k, v = heads(q), heads(k), heads(v)
    scale = SB_DH ** -0.5
    nb = S // SB_BLOCK
    qb = q.reshape(B, SB_HEADS, nb, SB_BLOCK, SB_DH).transpose(2, 0, 1, 3, 4)
    kpos = jnp.arange(S)

    def block(args):
        q_blk, b = args
        qpos = b * SB_BLOCK + jnp.arange(SB_BLOCK)
        z = jnp.einsum('bhqd,bhkd->bhqk', q_blk, k) * scale
        mask = (kpos[None, :] < qpos[:, None])[None, None]
        log_one_minus = jnp.where(mask, jax.nn.log_sigmoid(-z), 0.0)
        rem = lax.cumsum(log_one_minus, axis=3, reverse=True) - log_one_minus
        a = jnp.where(mask, jnp.exp(jax.nn.log_sigmoid(z) + rem), 0.0)
        return jnp.einsum('bhqk,bhkd->bhqd', a, v)

    o = lax.map(block, (qb, jnp.arange(nb)))
    o = o.transpose(1, 0, 3, 2, 4).reshape(B, S, SB_WIDTH)
    return o.astype(h.dtype) @ w_out

def first_inputs(seed: int = 0) -> dict:
    key = jax.random.key(seed)
    ks = jax.random.split(key, 16)
    f32 = jnp.float32
    def w(k, shape, fan_in):
        return jax.random.normal(k, shape, f32) * (fan_in ** -0.5)
    x = jax.random.normal(ks[0], (BATCH, SEQ, D_MODEL), f32)
    p = jax.random.normal(ks[1], (DEPTH, BATCH, SEQ, PLE_DIM), f32)
    positions = jnp.broadcast_to(jnp.arange(SEQ, dtype=jnp.int32), (BATCH, SEQ))
    norm_gains = 1.0 + 0.05 * jax.random.normal(ks[2], (DEPTH, N_NORMS, D_MODEL), f32)
    ffn_w_gate = w(ks[3], (DEPTH, 2, D_MODEL, D_FF), D_MODEL)
    ffn_w_up = w(ks[4], (DEPTH, 2, D_MODEL, D_FF), D_MODEL)
    ffn_w_down = w(ks[5], (DEPTH, 2, D_FF, D_MODEL), D_FF)
    ret_w_in = w(ks[6], (N_RET_LAYERS, D_MODEL, RET_IN), D_MODEL)
    ret_gn_gain = 1.0 + 0.05 * jax.random.normal(ks[7], (N_RET_LAYERS, RET_V), f32)
    ret_w_out = w(ks[8], (N_RET_LAYERS, RET_V, D_MODEL), RET_V)
    sb_w_in = w(ks[9], (N_SB_LAYERS, D_MODEL, SB_IN), D_MODEL)
    sb_w_out = w(ks[10], (N_SB_LAYERS, SB_WIDTH, D_MODEL), SB_WIDTH)
    ple_w_gate = w(ks[11], (DEPTH, D_MODEL, D_MODEL), D_MODEL)
    ple_w_proj = w(ks[12], (DEPTH, PLE_DIM, D_MODEL), PLE_DIM)
    return {"x": x, "p": p, "positions": positions, "norm_gains": norm_gains,
            "ffn_w_gate": ffn_w_gate, "ffn_w_up": ffn_w_up, "ffn_w_down": ffn_w_down,
            "ret_w_in": ret_w_in, "ret_gn_gain": ret_gn_gain, "ret_w_out": ret_w_out,
            "sb_w_in": sb_w_in, "sb_w_out": sb_w_out,
            "ple_w_gate": ple_w_gate, "ple_w_proj": ple_w_proj}

def first_block(x, p, positions, norm_gains, ffn_w_gate, ffn_w_up, ffn_w_down,
              ret_w_in, ret_gn_gain, ret_w_out, sb_w_in, sb_w_out,
              ple_w_gate, ple_w_proj):
    h = x
    for i in range(DEPTH):
        g = norm_gains[i]
        f = swiglu(rmsnorm(h, g[0]), ffn_w_gate[i, 0], ffn_w_up[i, 0], ffn_w_down[i, 0])
        h = h + FFN_RES_WEIGHT * rmsnorm(f, g[1])
        m_in = rmsnorm(h, g[2])
        j = i // N_MIXERS
        if i % N_MIXERS == 0:
            m = retention(m_in, positions, ret_w_in[j], ret_gn_gain[j], ret_w_out[j])
        else:
            m = stick_breaking(m_in, sb_w_in[j], sb_w_out[j])
        h = h + rmsnorm(m, g[3])
        f = swiglu(rmsnorm(h, g[4]), ffn_w_gate[i, 1], ffn_w_up[i, 1], ffn_w_down[i, 1])
        h = h + FFN_RES_WEIGHT * rmsnorm(f, g[5])
        gate = jax.nn.sigmoid(rmsnorm(h, g[6]) @ ple_w_gate[i])
        e = p[i] @ ple_w_proj[i]
        h = h + rmsnorm(gate * e, g[7])
    return h


CONV_WIDTH = D_MODEL
CONV_K = 3
N_HEADS = 16
HEAD_DIM = D_MODEL // N_HEADS
ATTN_WIDTH = N_HEADS * HEAD_DIM
MOBA_BLOCK = 256
MOBA_TOPK = 3
Q_CHUNK = 64
N_CONV_LAYERS = (DEPTH + 1) // 2
N_ATTN_LAYERS = DEPTH // 2
EPS = 1e-6
NEG = -1e30


def rms_norm(x, g):
    x32 = x.astype(jnp.float32)
    y = x32 * lax.rsqrt(jnp.mean(x32 * x32, axis=-1, keepdims=True) + EPS)
    return (y * g.astype(jnp.float32)).astype(x.dtype)

def alibi_slopes(n_heads):
    return jnp.asarray(2.0 ** (-8.0 * np.arange(1, n_heads + 1) / n_heads), dtype=jnp.float32)

def short_conv_mixer(h, w_in, conv_w, w_out):
    S = h.shape[1]
    b_gate, c_gate, xv, z = jnp.split(h @ w_in, 4, axis=-1)
    u = c_gate * xv
    u_pad = jnp.pad(u, ((0, 0), (CONV_K - 1, 0), (0, 0)))
    conv = conv_w[0] * u_pad[:, 0:S]
    for k in range(1, CONV_K):
        conv = conv + conv_w[k] * u_pad[:, k:k + S]
    y = b_gate * conv * jax.nn.silu(z)
    return y @ w_out

def moba_mixer(h, w_in, q_gain, k_gain, w_out):
    Bsz, S, _ = h.shape
    q, k, v, z = jnp.split(h @ w_in, 4, axis=-1)

    def heads(t):
        return t.reshape(Bsz, S, N_HEADS, HEAD_DIM).transpose(0, 2, 1, 3)

    q = rms_norm(heads(q), q_gain) * (HEAD_DIM ** -0.5)
    k = rms_norm(heads(k), k_gain)
    v = heads(v)

    n_blk = -(-S // MOBA_BLOCK)
    s_pad = n_blk * MOBA_BLOCK
    pad = ((0, 0), (0, 0), (0, s_pad - S), (0, 0))
    q, k, v = jnp.pad(q, pad), jnp.pad(k, pad), jnp.pad(v, pad)
    k_blocks = k.reshape(Bsz, N_HEADS, n_blk, MOBA_BLOCK, HEAD_DIM)
    v_blocks = v.reshape(Bsz, N_HEADS, n_blk, MOBA_BLOCK, HEAD_DIM)
    k_mean = jnp.mean(k_blocks.astype(jnp.float32), axis=3).astype(k.dtype)

    topk = min(MOBA_TOPK, n_blk)
    slopes = alibi_slopes(N_HEADS)
    n_chunk = s_pad // Q_CHUNK
    h_ar = jnp.arange(N_HEADS)[:, None, None]
    blk_ar = jnp.arange(n_blk)
    key_off = jnp.arange(MOBA_BLOCK)
    q_off = jnp.arange(Q_CHUNK)

    def chunk(i):
        b = i // n_chunk
        c = i % n_chunk
        t0 = c * Q_CHUNK
        qc = lax.dynamic_slice_in_dim(q[b], t0, Q_CHUNK, axis=1)
        kb = k_blocks[b]
        vb = v_blocks[b]
        q_blk = t0 // MOBA_BLOCK
        t_pos = t0 + q_off
        gate = jnp.einsum('hqd,hnd->hqn', qc, k_mean[b]).astype(jnp.float32)
        gate = jnp.where(blk_ar < q_blk, gate, NEG)
        _, idx = lax.top_k(gate, topk)
        valid = idx < q_blk
        k_sel = kb[h_ar, idx]
        v_sel = vb[h_ar, idx]
        s_past = jnp.einsum('hqd,hqjkd->hqjk', qc, k_sel).astype(jnp.float32)
        past_dist = (t_pos[None, :, None, None] - (idx[..., None] * MOBA_BLOCK + key_off)).astype(jnp.float32)
        s_past = s_past - slopes[:, None, None, None] * past_dist
        s_past = jnp.where(valid[..., None], s_past, NEG)
        k_own = lax.dynamic_index_in_dim(kb, q_blk, axis=1, keepdims=False)
        v_own = lax.dynamic_index_in_dim(vb, q_blk, axis=1, keepdims=False)
        own_dist = t_pos[:, None] - (q_blk * MOBA_BLOCK + key_off)[None, :]
        s_own = jnp.einsum('hqd,hkd->hqk', qc, k_own).astype(jnp.float32)
        s_own = jnp.where(own_dist[None] >= 0,
                          s_own - slopes[:, None, None] * own_dist.astype(jnp.float32)[None], NEG)
        n_past = topk * MOBA_BLOCK
        scores = jnp.concatenate([s_past.reshape(N_HEADS, Q_CHUNK, n_past), s_own], axis=-1)
        p = jax.nn.softmax(scores, axis=-1).astype(v.dtype)
        p_past = p[..., :n_past].reshape(N_HEADS, Q_CHUNK, topk, MOBA_BLOCK)
        p_own = p[..., n_past:]
        return (jnp.einsum('hqjk,hqjkd->hqd', p_past, v_sel)
                + jnp.einsum('hqk,hkd->hqd', p_own, v_own))

    out = lax.map(chunk, jnp.arange(Bsz * n_chunk))
    out = out.reshape(Bsz, n_chunk, N_HEADS, Q_CHUNK, HEAD_DIM).transpose(0, 1, 3, 2, 4)
    out = out.reshape(Bsz, s_pad, ATTN_WIDTH)[:, :S]
    y = out * jax.nn.silu(z)
    return y @ w_out

def second_inputs(seed: int = 0) -> dict:
    key = jax.random.key(seed)
    ks = jax.random.split(key, 10)
    f32 = jnp.float32
    x = jax.random.normal(ks[0], (BATCH, SEQ, D_MODEL), f32)
    norm_g = 1.0 + 0.02 * jax.random.normal(ks[1], (DEPTH, D_MODEL), f32)
    conv_w_in = jax.random.normal(ks[2], (N_CONV_LAYERS, D_MODEL, 4 * CONV_WIDTH), f32) * D_MODEL ** -0.5
    conv_w = jax.random.normal(ks[3], (N_CONV_LAYERS, CONV_K, CONV_WIDTH), f32) * CONV_K ** -0.5
    conv_w_out = jax.random.normal(ks[4], (N_CONV_LAYERS, CONV_WIDTH, D_MODEL), f32) * CONV_WIDTH ** -0.5
    attn_w_in = jax.random.normal(ks[5], (N_ATTN_LAYERS, D_MODEL, 4 * ATTN_WIDTH), f32) * D_MODEL ** -0.5
    q_norm_g = 1.0 + 0.02 * jax.random.normal(ks[6], (N_ATTN_LAYERS, HEAD_DIM), f32)
    k_norm_g = 1.0 + 0.02 * jax.random.normal(ks[7], (N_ATTN_LAYERS, HEAD_DIM), f32)
    attn_w_out = jax.random.normal(ks[8], (N_ATTN_LAYERS, ATTN_WIDTH, D_MODEL), f32) * ATTN_WIDTH ** -0.5
    return {"x": x, "norm_g": norm_g, "conv_w_in": conv_w_in, "conv_w": conv_w,
            "conv_w_out": conv_w_out, "attn_w_in": attn_w_in, "q_norm_g": q_norm_g,
            "k_norm_g": k_norm_g, "attn_w_out": attn_w_out}

def second_block(x, norm_g, conv_w_in, conv_w, conv_w_out, attn_w_in, q_norm_g, k_norm_g, attn_w_out):
    h = x
    for i in range(DEPTH):
        hn = rms_norm(h, norm_g[i])
        j = i // N_MIXERS
        if i % N_MIXERS == 0:
            h = h + short_conv_mixer(hn, conv_w_in[j], conv_w[j], conv_w_out[j])
        else:
            h = h + moba_mixer(hn, attn_w_in[j], q_norm_g[j], k_norm_g[j], attn_w_out[j])
    return h


def setup_inputs(seed=0):
    out = dict(first_inputs(seed))
    for name, value in second_inputs(seed + 1).items():
        if name != "x":
            out[name + "_2"] = value
    return out


def reference(
    x, p, positions, norm_gains, ffn_w_gate, ffn_w_up, ffn_w_down, ret_w_in, ret_gn_gain,
    ret_w_out, sb_w_in, sb_w_out, ple_w_gate, ple_w_proj, norm_g_2, conv_w_in_2, conv_w_2,
    conv_w_out_2, attn_w_in_2, q_norm_g_2, k_norm_g_2, attn_w_out_2,
):
    x = first_block(
        x, p, positions, norm_gains, ffn_w_gate, ffn_w_up, ffn_w_down, ret_w_in, ret_gn_gain,
        ret_w_out, sb_w_in, sb_w_out, ple_w_gate, ple_w_proj,
    )
    return second_block(
        x, norm_g_2, conv_w_in_2, conv_w_2, conv_w_out_2, attn_w_in_2, q_norm_g_2, k_norm_g_2,
        attn_w_out_2,
    )


_drawn_inputs = setup_inputs


def setup_inputs(seed=0):
    import zlib

    import numpy as np

    out = dict(_drawn_inputs(seed))
    spreads = {}
    factors = {'norm_g_2': 5.584, 'q_norm_g_2': 8.0, 'k_norm_g_2': 8.0}
    for name, (base, spread) in spreads.items():
        noise = np.random.default_rng([zlib.crc32(name.encode()), seed]).standard_normal(out[name].shape)
        drawn = base * np.exp(spread * noise) if base else spread * noise
        out[name] = __import__('jax').numpy.asarray(drawn.astype(out[name].dtype))
    for name, factor in factors.items():
        out[name] = (out[name] * factor).astype(out[name].dtype)
    return out
```

```python
from contextlib import ExitStack

import numpy as np

import concourse.bass as bass
from concourse import mybir

F32 = mybir.dt.float32
F32R = mybir.dt.float32r
I32 = mybir.dt.int32
ACT = mybir.ActivationFunctionType
ALU = mybir.AluOpType
AX_X = mybir.AxisListType.X

P = 128
SEQ = 256
NT = SEQ // P
D = 1024
DC = D // P
COLS = 512
SC = 2
RING = 8
RAW = 4
TURN_AHEAD = 2
BANKS = 4
F = 2816
FB = 256
FI = F // FB
FC = F // P
EPS = 1e-6
GN_EPS = 1e-5
RH, RDK, RDV = 4, 256, 512
SH, SDH = 8, 128
MH, MDH = 16, 64
NEG = -1e30
TWO_PI = 2.0 * np.pi

UPAD = SEQ + 2
MAGIC = 1.5 * 2.0 ** 23

HW_SILU, HW_HID, HW_P = 0, 512, 1024
EW_E, EW_S = 1536, 3584
RW_QK, RW_QKR, RW_QKT, RW_V, RW_G = 0, 1024, 2048, 3072, 4096
RW_P, RW_Y, RW_GN, RW_DECAY, RW_ROPE = 5120, 5504, 6528, 7040, 7296
SW_QK, SW_V, SW_QT, SW_KT, SW_HEAD = 0, 1024, 2048, 3072, 4096
SW_MASK, SW_NEG, SW_TRI, SW_ONES = 7168, 7552, 7936, 8064
CW_C, CW_X, CW_B, CW_Z, CW_U = 0, 1024, 2048, 3072, 4096
CW_Y = CW_U + 4 * UPAD

MW_Q, MW_K, MW_V, MW_Z, MW_QT, MW_KT = 0, 1024, 2048, 3072, 4096, 5120
MW_HEAD, MW_DIST, MW_SQ = 6144, 7680, 8064
AW_FREQ, AW_POS, AW_ANGLE, AW_K, AW_KH = 1536, 1664, 1792, 2048, 2304
WORK = 8700

_WIDTHS = [("ident", P), ("inv_freq", P), ("decay", RH * SEQ), ("sb_mask", 384), ("sb_neg", 384),
           ("tri", P), ("ones", P), ("dist", 384)]
CONST_AT = {}
_at = 0
for _name, _w in _WIDTHS:
    CONST_AT[_name] = (_at, _at + _w)
    _at += _w
CONST_COLS = _at


def constants():
    c = np.zeros((P, CONST_COLS), np.float32)
    r = np.arange(P)

    def put(name, a):
        lo, hi = CONST_AT[name]
        c[:, lo:hi] = a

    put("ident", np.eye(P))
    put("inv_freq", (np.float32(10000.0) ** (-np.arange(P, dtype=np.float32) / np.float32(P)))[None, :])
    key, query = r[:, None].astype(np.float64), np.arange(SEQ)[None, :].astype(np.float64)
    decay = []
    for h in range(RH):
        log_gamma = np.log1p(-(2.0 ** (-5.0 - h)))
        rel = query - key
        decay.append(np.where(rel >= 0, np.exp(np.maximum(rel, 0) * log_gamma), 0.0) * RDK ** -0.5)
    put("decay", np.concatenate(decay, 1))
    causal = (r[:, None] < r[None, :]).astype(np.float64)
    put("sb_mask", np.concatenate([-causal, -np.ones((P, P)), -causal], 1))
    put("sb_neg", np.concatenate([NEG * (1 - causal), np.zeros((P, P)), NEG * (1 - causal)], 1))
    put("tri", (r[:, None] >= r[None, :]))
    put("ones", 1.0)
    own = np.where(r[None, :] <= r[:, None], r[:, None] - r[None, :], 1e32)
    put("dist", np.concatenate([own, P + r[:, None] - r[None, :], own], 1))
    return c


def phase_list():
    ffn_in = ("in", FI, 4, 1, 1)
    down = ("out", FC, 0, 1, 1)
    return [
        ("ffn_in0", *ffn_in), ("down0", *down),
        ("ret_in", "in", 12, 4, 1, 0), ("ret_out", "out", 16, 0, 1, 1),
        ("ffn_in1", *ffn_in), ("down1", *down),
        ("ple_proj0", "in", 2, 1, 1, 0), ("ple_gate0", "out", 8, 0, 1, 0),
        ("ffn_in2", *ffn_in), ("down2", *down),
        ("sb_in", "in", 6, 4, 1, 0), ("sb_out", "out", 8, 0, 1, 1),
        ("ffn_in3", *ffn_in), ("down3", *down),
        ("ple_proj1", "in", 2, 1, 1, 0), ("ple_gate1", "out", 8, 0, 1, 0),
        ("conv_in", "in", 8, 4, 1, 0), ("conv_out", "out", 8, 0, 0, 0),
        ("moba_in", "in", 8, 4, 1, 0), ("moba_out", "out", 8, 0, 0, 0),
    ]


class Phase:

    def __init__(self, name, kind, n, per_block, act, dve):
        self.name, self.kind, self.n, self.per_block, self.act, self.dve = name, kind, n, per_block, act, dve
        self.slots = n * per_block if kind == "in" else n
        self.groups = 2 * n if kind == "in" else 4
        self.window = 0 if kind == "in" else 8 if name.startswith("ple") else 4 if n == 8 else 6


def make_plan():
    phases, slot, group, used, act, dve = {}, 0, 0, 0, BANKS, BANKS
    release = {}
    for row in phase_list():
        p = Phase(*row)
        p.slot0, p.group0, p.act0, p.dve0 = slot, group, act, dve
        for s in range(p.slots):
            if p.kind == "in" and s % p.per_block == p.per_block - 1:
                release[slot + s] = ("sums", group + 2 * (s // p.per_block) + 2)
            elif p.kind == "out" and s >= p.slots - 2:
                release[slot + s] = ("sums", group + 2 + (s - p.slots + 2) + 1)
            else:
                used += 1
                release[slot + s] = ("used", used)
        slot += p.slots
        group += p.groups
        act += p.act * p.groups
        dve += p.dve * p.groups
        phases[p.name] = p
    return phases, release, slot


PHASES, RELEASE, SLOTS = make_plan()

MOBA_BLOCKS = [(0, 0), (1, 0), (0, 1), (1, 1), (2, 0), (2, 1), (3, 0), (3, 1)]

Y_WRITES = [("ffn0", FI), ("ret", 2 * RH), ("ffn1", FI), ("ffn2", FI), ("sb", SH), ("ffn3", FI), ("conv", DC), ("moba", 4)]


def y_base(name):
    at = [n for n, _ in Y_WRITES].index(name)
    return sum(k for _, k in Y_WRITES[:at])


def ret_turned(head, i, y=False):
    return 4 * head + (2 if y else 0) + i + 1


def two_pi_parts():
    parts, rest = [], TWO_PI
    for _ in range(3):
        e = 11 - int(np.floor(np.log2(abs(rest))))
        part = float(np.round(rest * 2.0 ** e) / 2.0 ** e)
        parts.append(part)
        rest -= part
    return parts + [float(np.float32(rest))]


def reads_before(p, m, act):
    if m >= BANKS:
        return (p.act0 + p.act * (m - BANKS + 1)) if act else (p.dve0 + p.dve * (m - BANKS + 1))
    back, q = m - BANKS, p
    order = list(PHASES.values())
    while back < 0:
        at = order.index(q)
        if at == 0:
            return BANKS
        q = order[at - 1]
        back += q.groups
    return (q.act0 + q.act * (back + 1)) if act else (q.dve0 + q.dve * (back + 1))


def build(nc, x, p_in, positions, norm_gains, ffn_w_gate, ffn_w_up, ffn_w_down, ret_w_in, ret_gn_gain,
          ret_w_out, sb_w_in, sb_w_out, ple_w_gate, ple_w_proj, norm_g_2, conv_w_in_2, conv_w_2,
          conv_w_out_2, attn_w_in_2, q_norm_g_2, k_norm_g_2, attn_w_out_2, consts, out):
    with ExitStack() as ctx:
        def sb(name, shape, dt=F32):
            return ctx.enter_context(nc.sbuf_tensor(name, shape, dt))

        def sem(name):
            return ctx.enter_context(nc.semaphore(name))

        raw = sb("raw", [P, RAW, SC, COLS])
        w_hi = sb("w_hi", [P, RING, SC, COLS], F32R)
        w_lo = sb("w_lo", [P, RING, SC, COLS], F32R)
        h = sb("h", [P, NT, D])
        x_hi = sb("x_hi", [P, DC, SEQ], F32R)
        x_lo = sb("x_lo", [P, DC, SEQ], F32R)
        y_hi = sb("y_hi", [P, FC, SEQ], F32R)
        y_lo = sb("y_lo", [P, FC, SEQ], F32R)
        p_hi = sb("p_hi", [P, 2, SEQ], F32R)
        p_lo = sb("p_lo", [P, 2, SEQ], F32R)
        post_gain = sb("post_gain", [P, D])
        fg = sb("fg", [P, NT, 2, COLS])
        xg = sb("xg", [P, 2, COLS])
        junk = sb("junk", [P, D], mybir.dt.bfloat16)
        trig = sb("trig", [P, 2, NT, P])
        ident = sb("ident", [P, P])
        gains_a = sb("gains_a", [P, P])
        gains_b = sb("gains_b", [P, 42])
        neg_half = sb("neg_half", [P, 16])
        stat = sb("stat", [P, 136])
        work = sb("work", [P, WORK])

        sums = [ctx.enter_context(nc.psum_tensor(f"sums{i}", [P, COLS], F32)) for i in range(BANKS)]
        turn = [ctx.enter_context(nc.psum_tensor(f"turn{i}", [P, COLS], F32)) for i in range(4)]

        f_sq = stat[:, 0:4]
        h_sq = stat[:, 4:6]
        r_in = stat[:, 6:8]
        r_post = stat[:, 8:10]
        tmp_in = stat[:, 10:12]
        tmp_post = stat[:, 12:16]
        gn_stats = stat[:, 16:28]
        gn_mv = stat[:, 28:32]
        gn_r = stat[:, 32:34]
        gn_tmp = stat[:, 34:36]
        qk_sq = stat[:, 36:52]
        qk_tmp = stat[:, 52:68]
        qk_r = stat[:, 68:84]
        soft = stat[:, 84:132]
        pos_f = stat[:, 132:134]

        raw_loaded = [sem(f"raw_loaded{i}") for i in range(RAW)]
        hi_made, lo_made = sem("hi_made"), sem("lo_made")
        slot_used, sums_done = sem("slot_used"), sem("sums_done")
        act_read, dve_read = sem("act_read"), sem("dve_read")
        x_loaded, c_loaded, g_loaded, rope_loaded = [sem("x_loaded0"), sem("x_loaded1")], sem("c_loaded"), sem("g_loaded"), sem("rope_loaded")
        post_loaded, p_loaded = sem("post_loaded"), sem("p_loaded")
        gn_loaded, decay_loaded, mask_loaded = sem("gn_loaded"), sem("decay_loaded"), sem("mask_loaded")
        const_made = sem("const_made")
        gains_turned, gains_made = sem("gains_turned"), sem("gains_made")
        h_new, h_turned, xg_made = sem("h_new"), sem("h_turned"), sem("xg_made")
        x_hi_made, x_lo_made = sem("x_hi_made"), sem("x_lo_made")
        h_squared, r_in_made, r_post_made = sem("h_squared"), sem("r_in_made"), sem("r_post_made")
        pool_step = sem("pool_step")
        hid_turned = sem("hid_turned")
        y_hi_made, y_lo_made = sem("y_hi_made"), sem("y_lo_made")
        p_turned, p_hi_made, p_lo_made = sem("p_turned"), sem("p_hi_made"), sem("p_lo_made")
        gated, gated_sq, fg_made = sem("gated"), sem("gated_sq"), sem("fg_made")
        trig_step, trig_made, angle_made = sem("trig_step"), sem("trig_made"), sem("angle_made")
        out_sent = sem("out_sent")
        mx = {n: sem("mx_" + n) for n in (
            "roped", "rope_step", "turned", "flat", "scores", "weights", "mixed", "stats", "gn_r",
            "gn_step", "gate", "y", "y_step")}
        sbs = {n: sem("sb_" + n) for n in ("turned", "flat", "z", "log", "act_step", "dve_step", "loss", "rem", "a", "o")}
        cv = {n: sem("cv_" + n) for n in ("mul", "turned", "flat", "step", "y", "pad")}
        mb = {n: sem("mb_" + n) for n in (
            "sq", "sq_step", "r", "normed", "turned", "flat", "s", "t", "max", "negmax", "exp",
            "pt", "pt_flat", "o", "recip", "rows", "gated", "y_turned")}

        block = ctx.enter_context(nc.Block())

        boundaries = ["start", "down0", "ret_out", "down1", "ple_gate0", "down2", "sb_out", "down3",
                      "ple_gate1", "conv_out"]
        pre_gain = {}
        for name, (layer, j) in {"start": (0, 0), "down0": (0, 2), "ret_out": (0, 4), "down1": (0, 6),
                                 "ple_gate0": (1, 0), "down2": (1, 2), "sb_out": (1, 4), "down3": (1, 6)}.items():
            pre_gain[name] = gains_a[:, (layer * 8 + j) * 8:(layer * 8 + j) * 8 + 8]
        pre_gain["ple_gate1"] = gains_b[:, 0:8]
        pre_gain["conv_out"] = gains_b[:, 8:16]
        post = {"down0": (0, 1, 0.5), "ret_out": (0, 3, 1.0), "down1": (0, 5, 0.5), "ple_gate0": (0, 7, 1.0),
                "down2": (1, 1, 0.5), "sb_out": (1, 3, 1.0), "down3": (1, 5, 0.5), "ple_gate1": (1, 7, 1.0)}
        post_order = list(post)

        def lin(value, step, j):
            return value if j is None else j * step + value

        def wait_slot_free(eng, n, j=None):
            if n >= RING:
                kind, value = RELEASE[n - RING]
                if kind == "used":
                    eng.wait_ge(slot_used, lin(value, 6, j))
                else:
                    eng.wait_ge(sums_done, lin(value, 4, j))

        def mb_transposed(half):
            if half == 0:
                return work[:, MW_QT:MW_QT + 1024], work[:, MW_KT:MW_KT + 1024]
            rows = fg[:, :, :, :].rearrange("p t q n -> p (t q n)")
            return rows[:, 0:1024], rows[:, 1024:2048]

        def mb_values(half):
            rows = post_gain[:, :] if half else work[:, MW_V:MW_V + 1024]
            return rows.rearrange("p (t n) -> p t n", t=2)

        def mb_y_bank(half, i):
            return turn[0] if (half, i) == (1, 1) else turn[3]

        @block.sync
        def _(sp):
            def load_slot(n, parts, j=None):
                if n >= RAW:
                    sp.wait_ge(lo_made, lin(n - RAW + 1, RING, j))
                for dst, src in parts:
                    sp.dma_start(dst, src).then_inc(raw_loaded[n % RAW], 16)

            def plain(n, w, slot_row, col):
                load_slot(n, [(raw[:, n % RAW, c, :], w[(slot_row + c) * P:(slot_row + c + 1) * P, col:col + COLS])
                              for c in range(SC)])

            def out_weights(name, w, between=None):
                ph = PHASES[name]
                for s in range(ph.slots):
                    plain(ph.slot0 + s, w, (s // 2) * SC, (s % 2) * COLS)
                    if s == 4 and between:
                        between()

            def load_post(name):
                k = post_order.index(name)
                if k:
                    before = post_order[k - 1]
                    if before.startswith("ple"):
                        sp.wait_ge(fg_made, 4 * (int(before[-1]) + 1))
                    else:
                        sp.wait_ge(dve_read, PHASES[before].dve0 + 4)
                layer, j, _ = post[name]
                sp.dma_start(post_gain[:, :], norm_gains[layer, j, :].partition_broadcast(P)).then_inc(post_loaded, 16)

            def ffn_weights(f):
                layer, half = f // 2, f % 2
                gate = ffn_w_gate[layer, half].rearrange("(c p) n -> p c n", p=P)
                up = ffn_w_up[layer, half].rearrange("(c p) n -> p c n", p=P)
                ph = PHASES[f"ffn_in{f}"]

                def parts(n, s, col):
                    return [(raw[:, n % RAW, :, 0:FB], gate[:, SC * s:SC * s + SC, col]),
                            (raw[:, n % RAW, :, FB:2 * FB], up[:, SC * s:SC * s + SC, col])]

                for s in range(4):
                    load_slot(ph.slot0 + s, parts(ph.slot0 + s, s, slice(0, FB)))
                if f == 0:
                    load_rope()
                with sp.Fori(0, (FI - 1) // 2) as j:
                    for s in range(8):
                        n = ph.slot0 + 4 + s
                        load_slot(n, parts(n, s % 4, bass.ds(j * (2 * FB) + FB * (1 + s // 4), FB)), j)
                load_post(f"down{f}")
                if f % 2:
                    if f == 3:
                        sp.wait_ge(p_turned, 1)
                    for t in range(NT):
                        sp.dma_start(work[:, 1024 + 256 * t:1280 + 256 * t], p_in[layer, 0, t * P:(t + 1) * P, :]).then_inc(p_loaded, 16)
                out_weights(f"down{f}", ffn_w_down[layer, half])

            def in_weights(name, w, cols, between=None):
                ph = PHASES[name]
                for b, col in enumerate(cols):
                    if b == 2 and between:
                        between()
                    for s in range(ph.per_block):
                        plain(ph.slot0 + b * ph.per_block + s, w, SC * s, col)

            c0, c1 = CONST_AT["ident"]
            sp.dma_start(ident[:, :], consts[:, c0:c1]).then_inc(c_loaded, 16)
            sp.dma_start(h[:, 0, :], x[0, 0:P, :]).then_inc(x_loaded[0], 16)
            sp.dma_start(work[:, 0:P], norm_gains.rearrange("l j (c p) -> (l j c) p", p=P)).then_inc(g_loaded, 16)
            sp.dma_start(work[0:16, P:2 * P], norm_g_2.rearrange("l (c p) -> (l c) p", p=P)).then_inc(g_loaded, 16)
            sp.dma_start(work[16:40, P:2 * P], conv_w_2[0].rearrange("k (c p) -> (k c) p", p=P)).then_inc(g_loaded, 16)
            for row, gain in ((40, q_norm_g_2), (41, k_norm_g_2)):
                for half in range(2):
                    sp.dma_start(work[row:row + 1, P + MDH * half:P + MDH * (half + 1)], gain).then_inc(g_loaded, 16)
            sp.dma_start(h[:, 1, :], x[0, P:2 * P, :]).then_inc(x_loaded[1], 16)

            def load_rope():
                c0, c1 = CONST_AT["inv_freq"]
                sp.dma_start(work[:, AW_FREQ:AW_FREQ + P], consts[:, c0:c1]).then_inc(rope_loaded, 16)
                for t in range(NT):
                    sp.dma_start(work[:, AW_POS + t:AW_POS + t + 1].bitcast(I32),
                                 positions[0:1, t * P:(t + 1) * P].rearrange("a p -> p a")).then_inc(rope_loaded, 16)

            ffn_weights(0)

            ph = PHASES["ret_in"]
            w = ret_w_in[0].rearrange("(c p) n -> p c n", p=P)
            for hd in range(RH):
                for s in range(4):
                    n = ph.slot0 + 12 * hd + s
                    load_slot(n, [(raw[:, n % RAW, :, i * RDK:(i + 1) * RDK],
                                   w[:, SC * s:SC * s + SC, i * D + hd * RDK:i * D + (hd + 1) * RDK]) for i in range(2)])
                for b in range(2):
                    for s in range(4):
                        plain(ph.slot0 + 12 * hd + 4 + 4 * b + s, ret_w_in[0], SC * s, 2 * D + 2 * D * b + hd * RDV)
                    if b == 0:
                        if hd:
                            sp.wait_ge(mx["gate"], 2 * hd)
                            sp.wait_ge(mx["weights"], 2 * hd)
                        sp.dma_start(work[:, RW_GN:RW_GN + 512],
                                     ret_gn_gain[0, hd * RDV:(hd + 1) * RDV].partition_broadcast(P)).then_inc(gn_loaded, 16)
                        c0 = CONST_AT["decay"][0] + hd * SEQ
                        sp.dma_start(work[:, RW_DECAY:RW_DECAY + SEQ], consts[:, c0:c0 + SEQ]).then_inc(decay_loaded, 16)
            load_post("ret_out")
            out_weights("ret_out", ret_w_out[0])

            for layer in range(2):
                if layer:
                    ffn_weights(2)
                    sp.wait_ge(hid_turned, 3 * FI)
                    sp.dma_start(work[:, SW_MASK:SW_MASK + 1024],
                                 consts[:, CONST_AT["sb_mask"][0]:CONST_AT["ones"][1]]).then_inc(mask_loaded, 16)
                    in_weights("sb_in", sb_w_in[0], [i * D + COLS * half for half in range(2) for i in range(3)])
                    load_post("sb_out")
                    out_weights("sb_out", sb_w_out[0])
                ffn_weights(1 + 2 * layer)
                in_weights(f"ple_proj{layer}", ple_w_proj[layer], [0, COLS])
                out_weights(f"ple_gate{layer}", ple_w_gate[layer], lambda: load_post(f"ple_gate{layer}"))

            in_weights("conv_in", conv_w_in_2[0], [i * D + COLS * half for half in range(2) for i in (1, 2, 0, 3)])
            out_weights("conv_out", conv_w_out_2[0])
            def load_dist():
                sp.wait_ge(cv["y"], DC)
                sp.dma_start(work[:, MW_DIST:MW_DIST + 384],
                             consts[:, CONST_AT["dist"][0]:CONST_AT["dist"][1]]).then_inc(mask_loaded, 16)

            in_weights("moba_in", attn_w_in_2[0], [i * D + COLS * half for i, half in MOBA_BLOCKS], load_dist)
            out_weights("moba_out", attn_w_out_2[0])
            for t in range(NT):
                sp.wait_ge(h_new, 4 * len(boundaries) - 4 + 2 * t + 2)
                sp.dma_start(out[0, t * P:(t + 1) * P, :], h[:, t, :]).then_inc(out_sent, 16)
            sp.wait_ge(out_sent, 16 * NT)

        @block.tensor
        def _(pe):
            def products(bank, t, n, j, c0, hi, lo, first, last, sign):
                pe.wait_ge(lo_made, lin(n + 1, RING, j))
                rows = slice(t * P, (t + 1) * P)
                for c in range(SC):
                    a, b = hi[:, c0 + c, rows], lo[:, c0 + c, rows]
                    wh, wl = w_hi[:, n % RING, c, :], w_lo[:, n % RING, c, :]
                    pe.matmul(bank[:, :], a, wh, start=(first and c == 0), stop=False, skip_group_check=True)
                    pe.matmul(bank[:, :], a, wl, start=False, stop=False, skip_group_check=True)
                    mm = pe.matmul(bank[:, :], b, wh, start=False, stop=(last and c == SC - 1), skip_group_check=True)
                if sign is not None:
                    mm.then_inc(sign, 1)

            def wait_bank(ph, m, j=None, start=None):
                if j is None:
                    pe.wait_ge(act_read, reads_before(ph, m, True))
                    pe.wait_ge(dve_read, reads_before(ph, m, False))
                else:
                    pe.wait_ge(act_read, lin(ph.act0 + ph.act * (m - 3), 4 * ph.act, j))
                    pe.wait_ge(dve_read, lin(ph.dve0 + ph.dve * (m - 3), 4 * ph.dve, j))

            def group(ph, m, hi, lo, j=None, hook=None, new_x=None):
                wait_bank(ph, m, j)
                t, per = m % 2, ph.per_block
                for s in range(per):
                    n = ph.slot0 + (m // 2) * per + s
                    if new_x is not None:
                        pe.wait_ge(x_lo_made, 4 * new_x + 2 * t + (2 * s) // per + 1)
                    last = s == per - 1
                    sign = sums_done if last else (slot_used if t == 1 else None)
                    products(sums[(ph.group0 + m) % BANKS], t, n, j, SC * s, hi, lo, s == 0, last, sign)
                    if hook and s == per - 2:
                        hook()

            def turn_h(b, t):
                for q in range(2):
                    if b == 0:
                        pe.wait_ge(x_loaded[t], 16)
                    else:
                        pe.wait_ge(h_new, 4 * (b - 1) + 2 * t + q + 1)
                    for c in range(4):
                        mm = pe.transpose(turn[2 * t + q][:, c * P:(c + 1) * P],
                                          h[:, t, (4 * q + c) * P:(4 * q + c + 1) * P], ident[:, :])
                    mm.then_inc(h_turned, 1)

            def wait_x(b, t):
                pe.wait_ge(x_lo_made, 4 * b + 2 * t + 2)

            def in_proj(name, b, hooks):
                ph = PHASES[name]
                for m in range(ph.groups):
                    group(ph, m, x_hi, x_lo, hook=(lambda: turn_h(b, 1)) if m == 0 else None,
                          new_x=b if m < 2 else None)
                    if m in hooks:
                        hooks[m]()

            def out_proj(name, b, hi, lo, waits, hooks):
                ph = PHASES[name]
                ws = ph.slots - ph.window
                opened = set()

                def part(s, t):
                    g = 2 * t + s % 2
                    if s < 2:
                        wait_bank(ph, g)
                    for key in (s, (s, t)):
                        if key in waits:
                            waits[key]()
                    last = s >= ph.slots - 2
                    sign = sums_done if last else (slot_used if t == 1 else None)
                    products(sums[(ph.group0 + g) % BANKS], t, ph.slot0 + s, None, SC * (s // 2), hi, lo,
                             g not in opened, last, sign)
                    opened.add(g)

                for s in range(ws):
                    for t in range(NT):
                        part(s, t)
                    if s in hooks:
                        hooks[s]()
                for s in range(ws, ph.slots):
                    part(s, 0)
                for s in range(ws, ph.slots):
                    if s == ph.slots - TURN_AHEAD and b is not None:
                        turn_h(b, 0)
                    part(s, 1)

            def turn_hidden(i):
                for c in range(2):
                    for t in range(NT):
                        mm = pe.transpose(turn[0][:, c * SEQ + t * P:c * SEQ + (t + 1) * P],
                                          work[:, 512 + t * FB + c * P:512 + t * FB + (c + 1) * P], ident[:, :])
                mm.then_inc(hid_turned, 1)

            def ffn(f, b):
                ph = PHASES[f"ffn_in{f}"]
                group(ph, 0, x_hi, x_lo, hook=lambda: turn_h(b, 1), new_x=b)
                group(ph, 1, x_hi, x_lo, new_x=b)
                with pe.Fori(0, (FI - 1) // 2) as j:
                    for s in range(2):
                        group(ph, 2 + 2 * s, x_hi, x_lo, j)
                        pe.wait_ge(dve_read, lin(ph.dve0 + 2 * s + 2, 4, j))
                        turn_hidden(s)
                        group(ph, 3 + 2 * s, x_hi, x_lo, j)

                def last_hidden():
                    pe.wait_ge(dve_read, ph.dve0 + 2 * FI)
                    turn_hidden(FI - 1)
                    if f % 2:
                        pe.wait_ge(p_loaded, 32 * (f // 2 + 1))
                        for c in range(2):
                            for t in range(NT):
                                mm = pe.transpose(turn[1][:, c * SEQ + t * P:c * SEQ + (t + 1) * P],
                                                  work[:, 1024 + 256 * t + c * P:1024 + 256 * t + (c + 1) * P], ident[:, :])
                        mm.then_inc(p_turned, 1)

                def rows(count):
                    return lambda: pe.wait_ge(y_lo_made, count)

                out_proj(f"down{f}", b + 1, y_hi, y_lo,
                         {0: rows(y_base(f"ffn{f}") + FI - 1), FC - 2: rows(y_base(f"ffn{f}") + FI)}, {1: last_hidden})

            pe.wait_ge(c_loaded, 16)
            pe.wait_ge(g_loaded, 16 * 7)
            pe.transpose(turn[2][:, 0:P], work[:, 0:P], ident[:, :])
            pe.transpose(turn[2][:, P:P + 42], work[0:42, P:2 * P], ident[0:42, 0:42]).then_inc(gains_turned, 1)
            turn_h(0, 0)
            pe.wait_ge(gains_made, 1)

            ffn(0, 0)

            def ret_turn_qk(hd):
                pe.wait_ge(mx["roped"], 2 * hd + 2)
                pe.wait_ge(y_lo_made, y_base("ret") + 2 * hd)
                for i in range(2):
                    for c in range(2):
                        for t in range(NT):
                            mm = pe.transpose(turn[i][:, c * SEQ + t * P:c * SEQ + (t + 1) * P],
                                              work[:, RW_QKR + t * 512 + i * RDK + c * P:RW_QKR + t * 512 + i * RDK + (c + 1) * P],
                                              ident[:, :])
                    mm.then_inc(mx["turned"], 1)

            def ret_scores(hd):
                pe.wait_ge(mx["flat"], 2 * hd + 2)
                if hd:
                    pe.wait_ge(mx["y"], 2 * hd)
                q = work[:, RW_QKT:RW_QKT + 512].rearrange("p (c t) -> p c t", c=2)
                k = work[:, RW_QKT + 512:RW_QKT + 1024].rearrange("p (c t) -> p c t", c=2)
                for kb in range(2):
                    lo = kb * P
                    for c in range(2):
                        mm = pe.matmul(turn[2][:, kb * SEQ:kb * SEQ + SEQ - lo], k[:, c, lo:lo + P], q[:, c, lo:SEQ],
                                       start=(kb == 0 and c == 0), stop=(c == 1), skip_group_check=True)
                mm.then_inc(mx["scores"], 1)

            def ret_mix(hd):
                pe.wait_ge(mx["weights"], 2 * hd + 2)
                pe.wait_ge(act_read, PHASES["ret_in"].act0 + 6 * hd + 4)
                v = work[:, RW_V:RW_V + 1024].rearrange("p (t n) -> p t n", t=2)
                w = work[:, RW_P:RW_P + 384]
                pe.matmul(turn[3][:, :], w[:, 0:P], v[:, 0, :], start=True, stop=True).then_inc(mx["mixed"], 1)
                pe.matmul(turn[2][:, :], w[:, P:2 * P], v[:, 0, :], start=True, stop=False)
                pe.matmul(turn[2][:, :], w[:, 2 * P:3 * P], v[:, 1, :], start=False, stop=True).then_inc(mx["mixed"], 1)

            def ret_turn_y(hd):
                pe.wait_ge(mx["y"], 2 * hd + 2)
                for i in range(2):
                    for c in range(2):
                        for t in range(NT):
                            mm = pe.transpose(turn[i][:, c * SEQ + t * P:c * SEQ + (t + 1) * P],
                                              work[:, RW_Y + t * 512 + (2 * i + c) * P:RW_Y + t * 512 + (2 * i + c + 1) * P],
                                              ident[:, :])
                    mm.then_inc(mx["turned"], 1)

            hooks = {}
            for hd in range(RH):
                if hd:
                    hooks[6 * hd] = lambda hd=hd: ret_turn_y(hd - 1)
                hooks[6 * hd + 2] = lambda hd=hd: ret_turn_qk(hd)
                hooks[6 * hd + 3] = lambda hd=hd: ret_scores(hd)
                hooks[6 * hd + 4] = lambda hd=hd: ret_mix(hd)
            in_proj("ret_in", 1, hooks)
            yb = y_base("ret")
            out_proj("ret_out", 2, y_hi, y_lo,
                     {0: lambda: pe.wait_ge(y_lo_made, yb + 6), 12: lambda: pe.wait_ge(y_lo_made, yb + 7),
                      14: lambda: pe.wait_ge(y_lo_made, yb + 8)}, {1: lambda: ret_turn_y(RH - 1)})

            def ple(layer, b):
                ph = PHASES[f"ple_proj{layer}"]
                pe.wait_ge(p_lo_made, layer + 1)
                for m in range(ph.groups):
                    group(ph, m, p_hi, p_lo)
                    if m == 2:
                        turn_h(b, 1)
                out_proj(f"ple_gate{layer}", b + 1, x_hi, x_lo, {(0, 0): lambda: wait_x(b, 0), (0, 1): lambda: wait_x(b, 1)}, {})

            ffn(1, 2)
            ple(0, 3)
            ffn(2, 4)

            def sb_turn(which, half, base):
                pe.wait_ge(act_read, PHASES["sb_in"].act0 + base)
                for i in range(2):
                    for hd in range(2):
                        for t in range(NT):
                            mm = pe.transpose(turn[2 * which + i][:, hd * SEQ + t * P:hd * SEQ + (t + 1) * P],
                                              work[:, SW_QK + t * 512 + (2 * i + hd) * P:SW_QK + t * 512 + (2 * i + hd + 1) * P],
                                              ident[:, :])
                    mm.then_inc(sbs["turned"], 1)

            def sb_z(hd):
                half, k = hd // 4, hd % 4
                pe.wait_ge(sbs["flat"], 4 * half + 4)
                qT = work[:, SW_QT + k * SEQ:SW_QT + (k + 1) * SEQ]
                kT = work[:, SW_KT + k * SEQ:SW_KT + (k + 1) * SEQ]
                pe.matmul(turn[k][:, 0:SEQ], kT[:, 0:P], qT, start=True, stop=False, skip_group_check=True)
                pe.matmul(turn[k][:, SEQ:384], kT[:, P:SEQ], qT[:, P:SEQ], start=False, stop=False,
                          skip_group_check=True).then_inc(sbs["z"], 1)

            def sb_rem(hd):
                k = hd % 4
                pe.wait_ge(sbs["loss"], hd + 1)
                loss = work[:, SW_HEAD + (hd % 4) * 768 + 384:SW_HEAD + (hd % 4) * 768 + 768]
                tri, ones = work[:, SW_TRI:SW_TRI + P], work[:, SW_ONES:SW_ONES + P]
                kw = dict(start=False, skip_group_check=True)
                pe.matmul(turn[k][:, 0:SEQ], tri, loss[:, 0:SEQ], stop=False, **kw)
                pe.matmul(turn[k][:, SEQ:384], tri, loss[:, SEQ:384], stop=False, **kw)
                pe.matmul(turn[k][:, P:SEQ], ones, loss[:, SEQ:384], stop=False, **kw)
                pe.matmul(turn[k][:, 0:384], ident[:, :], work[:, SW_NEG:SW_NEG + 384], stop=True, **kw).then_inc(sbs["rem"], 1)

            def sb_mix(hd):
                half, k = hd // 4, hd % 4
                pe.wait_ge(sbs["a"], hd + 1)
                a = work[:, SW_HEAD + k * 768:SW_HEAD + k * 768 + 384]
                v = work[:, SW_V:SW_V + 1024].rearrange("p (t n) -> p t n", t=2)
                pe.matmul(turn[k][:, 0:SEQ], v[:, 0, k * P:(k + 1) * P], a[:, 0:SEQ], start=True, stop=False, skip_group_check=True)
                pe.matmul(turn[k][:, P:SEQ], v[:, 1, k * P:(k + 1) * P], a[:, SEQ:384], start=False, stop=True,
                          skip_group_check=True).then_inc(sbs["o"], 1)

            def sb_do(fn, heads):
                for hd in heads:
                    fn(hd)

            def after_v0():
                pe.wait_ge(mask_loaded, 16)
                sb_do(sb_z, range(4))

            hooks = {
                2: lambda: sb_turn(0, 0, 2), 4: lambda: sb_turn(1, 0, 4), 5: after_v0,
                6: lambda: sb_do(sb_rem, range(2)), 7: lambda: (sb_do(sb_rem, range(2, 4)), sb_do(sb_mix, range(2))),
                8: lambda: (sb_do(sb_mix, range(2, 4)), pe.wait_ge(y_lo_made, y_base("sb") + 2), sb_turn(0, 1, 8)),
                9: lambda: (pe.wait_ge(y_lo_made, y_base("sb") + 4), sb_turn(1, 1, 10)),
                10: lambda: sb_do(sb_z, range(4, 8)),
            }
            in_proj("sb_in", 5, hooks)
            yb2 = y_base("sb")
            out_proj("sb_out", 6, y_hi, y_lo,
                     {0: lambda: pe.wait_ge(y_lo_made, yb2 + 4), 4: lambda: pe.wait_ge(y_lo_made, yb2 + 6),
                      6: lambda: pe.wait_ge(y_lo_made, yb2 + 8)},
                     {1: lambda: sb_do(sb_rem, range(4, 8)), 3: lambda: sb_do(sb_mix, range(4, 8))})

            ffn(3, 6)
            ple(1, 7)

            def cv_turn(which, half):
                pe.wait_ge(cv["mul"], 4 * half + 2 * which + 2)
                if half:
                    pe.wait_ge(cv["flat"], 2) if which == 0 else pe.wait_ge(cv["y"], 4)
                for i in range(2):
                    for c in range(2):
                        for t in range(NT):
                            at = (CW_C if which == 0 else CW_B) + t * 512 + (2 * i + c) * P
                            mm = pe.transpose(turn[2 * which + i][:, c * SEQ + t * P:c * SEQ + (t + 1) * P],
                                              work[:, at:at + P], ident[:, :])
                    mm.then_inc(cv["turned"], 1)

            in_proj("conv_in", 8, {5: lambda: cv_turn(0, 0), 9: lambda: cv_turn(1, 0), 13: lambda: cv_turn(0, 1)})
            yb3 = y_base("conv")
            out_proj("conv_out", 9, y_hi, y_lo,
                     {0: lambda: pe.wait_ge(y_lo_made, yb3 + 4), 4: lambda: pe.wait_ge(y_lo_made, yb3 + 6),
                      6: lambda: pe.wait_ge(y_lo_made, yb3 + 8)}, {1: lambda: cv_turn(1, 1)})

            def mb_turn(which, half):
                at = (MW_Q, MW_K)[which]
                pe.wait_ge(mb["normed"], 4 * half + 2 * which + 2)
                if half:
                    pe.wait_ge(mb["flat"], 2 * which + 2)
                for i in range(2):
                    for c in range(2):
                        for t in range(NT):
                            mm = pe.transpose(turn[2 * which + i][:, c * SEQ + t * P:c * SEQ + (t + 1) * P],
                                              work[:, at + t * 512 + (2 * i + c) * P:at + t * 512 + (2 * i + c + 1) * P],
                                              ident[:, :])
                    mm.then_inc(mb["turned"], 1)

            def mb_scores(hd):
                half, k = hd // 8, hd % 8
                pe.wait_ge(mb["flat"], 8 if half else 6)
                if hd >= 2:
                    pe.wait_ge(mb["t"], hd - 1)
                c, r = k // 2, slice((k % 2) * MDH, (k % 2 + 1) * MDH)
                q, k_t = mb_transposed(half)
                qT = q[r, c * SEQ:(c + 1) * SEQ]
                kT = k_t[r, c * SEQ:(c + 1) * SEQ]
                b = turn[hd % 2]
                pe.matmul(b[:, 0:P], qT[:, 0:P], kT[:, 0:P], start=True, stop=True, skip_group_check=True)
                pe.matmul(b[:, P:384], qT[:, P:SEQ], kT[:, 0:SEQ], start=False, stop=True, skip_group_check=True).then_inc(mb["s"], 1)

            def mb_turn_p(hd):
                pe.wait_ge(mb["exp"], 2 * hd + 2)
                if hd:
                    pe.wait_ge(mb["pt_flat"], hd)
                else:
                    pe.wait_ge(mb["flat"], 8)
                at = MW_HEAD + (hd % 2) * 768
                for c in range(3):
                    mm = pe.transpose(turn[2][:, c * P:(c + 1) * P], work[:, at + c * P:at + (c + 1) * P], ident[:, :])
                mm.then_inc(mb["pt"], 1)

            def mb_mix(hd):
                half = hd // 8
                pe.wait_ge(mb["pt_flat"], hd + 1)
                pe.wait_ge(act_read, PHASES["moba_in"].act0 + 10 + 2 * half)
                at = MW_HEAD + (hd % 2) * 768 + 384
                v = mb_values(half)
                cols = slice((hd % 8) * MDH, (hd % 8 + 1) * MDH)
                b = turn[hd % 2][:, 384:512]
                pe.matmul(b[:, 0:MDH], work[:, at:at + P], v[:, 0, cols], start=True, stop=True, skip_group_check=True)
                pe.matmul(b[:, MDH:2 * MDH], work[:, at + P:at + 2 * P], v[:, 0, cols], start=False, stop=False, skip_group_check=True)
                pe.matmul(b[:, MDH:2 * MDH], work[:, at + 2 * P:at + 3 * P], v[:, 1, cols], start=False, stop=True,
                          skip_group_check=True).then_inc(mb["o"], 1)

            def mb_stage(k):
                for i, fn in ((0, mb_scores), (2, mb_mix), (1, mb_turn_p)):
                    if 0 <= k - i < MH // 2:
                        for hd in range(2):
                            if fn is mb_mix and k - i >= MH // 2 - 2:
                                pe.wait_ge(mb["t"], MH)
                                pe.wait_ge(mb["rows"], 2 * (2 * (k - i) + hd) - 2)
                            fn(2 * (k - i) + hd)

            def mb_turn_y(half, i):
                pe.wait_ge(mb["gated"], 2 * half + 2)
                bank = mb_y_bank(half, i)
                if (half, i) == (0, 0):
                    pe.wait_ge(mb["flat"], 8)
                elif (half, i) != (1, 1):
                    pe.wait_ge(y_lo_made, y_base("moba") + 2 * half + i)
                at = (MW_Q, MW_K)[half]
                for c in range(2):
                    for t in range(NT):
                        mm = pe.transpose(bank[:, c * SEQ + t * P:c * SEQ + (t + 1) * P],
                                          work[:, at + t * 512 + (2 * i + c) * P:at + t * 512 + (2 * i + c + 1) * P],
                                          ident[:, :])
                mm.then_inc(mb["y_turned"], 1)

            yb4 = y_base("moba")
            hooks = {3: lambda: mb_turn(0, 0), 5: lambda: mb_turn(1, 0), 7: lambda: mb_turn(0, 1),
                     8: lambda: mb_stage(0), 9: lambda: (mb_turn(1, 1), mb_stage(1)),
                     14: lambda: (mb_stage(6), mb_turn_y(0, 0)), 15: lambda: (mb_stage(7), mb_turn_y(0, 1))}
            hooks.update({8 + k: lambda k=k: mb_stage(k) for k in range(2, 6)})
            in_proj("moba_in", 9, hooks)
            out_proj("moba_out", None, y_hi, y_lo,
                     {0: lambda: pe.wait_ge(y_lo_made, yb4 + 1), 2: lambda: pe.wait_ge(y_lo_made, yb4 + 2),
                      4: lambda: pe.wait_ge(y_lo_made, yb4 + 3), 6: lambda: pe.wait_ge(y_lo_made, yb4 + 4)},
                     {0: lambda: mb_stage(8), 1: lambda: mb_stage(9), 3: lambda: (mb_turn_y(1, 0), mb_turn_y(1, 1))})

        @block.gpsimd
        def _(pool):
            pool.memset(neg_half[:, :], -0.5).then_inc(const_made, 1)
            pool.wait_ge(const_made, 1)
            step = [0]

            def rsqrt(dst, src, tmp, scale, eps, sign):
                k = src.shape[-1]
                pool.tensor_scalar(tmp, src, scale, eps, ALU.mult, ALU.add).then_inc(pool_step, 1)
                step[0] += 1
                pool.wait_ge(pool_step, step[0])
                pool.tensor_tensor(dst, tmp, neg_half[:, 0:k], ALU.pow).then_inc(sign, 1)

            def norm_in(b, t):
                pool.wait_ge(h_squared, 2 * b + t + 1)
                rsqrt(r_in[:, t:t + 1], h_sq[:, t:t + 1], tmp_in[:, t:t + 1], 1.0 / D, EPS, r_in_made)

            def norm_post(name, t):
                weight = post[name][2]
                ph = PHASES[name]
                if name.startswith("ple"):
                    pool.wait_ge(gated_sq, 4 * int(name[-1]) + 2 * t + 2)
                else:
                    pool.wait_ge(act_read, ph.act0 + 2 * t + 2)
                pool.tensor_tensor(tmp_post[:, 2 * t:2 * t + 1], f_sq[:, 2 * t:2 * t + 1], f_sq[:, 2 * t + 1:2 * t + 2],
                                   ALU.add).then_inc(pool_step, 1)
                step[0] += 1
                pool.wait_ge(pool_step, step[0])
                rsqrt(r_post[:, t:t + 1], tmp_post[:, 2 * t:2 * t + 1], tmp_post[:, 2 * t + 1:2 * t + 2],
                      1.0 / D / weight ** 2, EPS / weight ** 2, r_post_made)

            for t in range(NT):
                norm_in(0, t)
            for b, name in enumerate(boundaries[1:], 1):
                if name == "ret_out":
                    for k in range(2 * RH):
                        pool.wait_ge(mx["stats"], k + 1)
                        rsqrt(gn_r[:, k % 2:k % 2 + 1], gn_mv[:, 2 * (k % 2) + 1:2 * (k % 2) + 2],
                              gn_tmp[:, k % 2:k % 2 + 1], 1.0, GN_EPS, mx["gn_r"])
                for t in range(NT):
                    if name in post:
                        norm_post(name, t)
                    norm_in(b, t)
            for k in range(4):
                pool.wait_ge(mb["sq"], 2 * k + 2)
                rsqrt(qk_r, qk_sq, qk_tmp, 1.0 / MDH, EPS, mb["r"])

        @block.scalar
        def _(act):
            split_next = [0]
            junk_written = []

            def squared(sem, value):
                if junk_written:
                    act.wait_ge(*junk_written[-1])
                junk_written.append((sem, value))

            def split(n, j=None):
                act.wait_ge(raw_loaded[n % RAW], lin(32 * (n // RAW + 1), 64, j))
                wait_slot_free(act, n, j)
                act.activation(w_hi[:, n % RING].rearrange("p c n -> p (c n)"),
                               raw[:, n % RAW].rearrange("p c n -> p (c n)"), ACT.Copy).then_inc(hi_made, 1)

            def split_to(n):
                while split_next[0] < min(n, SLOTS):
                    split(split_next[0])
                    split_next[0] += 1

            def x_part(b, t):
                for q in range(2):
                    act.wait_ge(xg_made, 4 * b + 2 * t + q + 1)
                    act.activation(x_hi[:, 4 * q:4 * q + 4, t * P:(t + 1) * P],
                                   xg[:, q, :].rearrange("p (c t) -> p c t", c=4), ACT.Copy).then_inc(x_hi_made, 1)
                act.wait_ge(h_new, 4 * (b - 1) + 2 * t + 2) if b else act.wait_ge(x_loaded[t], 16)
                squared(h_squared, 2 * b + t + 1)
                act.activation(junk[:, :], h[:, t, :], ACT.Square, accum_out=h_sq[:, t:t + 1]).then_inc(h_squared, 1)

            def squares(name, t):
                ph = PHASES[name]
                for n in range(2):
                    act.wait_ge(sums_done, ph.group0 + 2 * t + n + 1)
                    squared(act_read, ph.act0 + 2 * t + n + 1)
                    act.activation(junk[:, 0:COLS], sums[(ph.group0 + 2 * t + n) % BANKS][:, :], ACT.Square,
                                   accum_out=f_sq[:, 2 * t + n:2 * t + n + 1]).then_inc(act_read, 1)

            def out_phase(name, b, late, read):
                ph = PHASES[name]
                base, free = ph.slot0, ph.slot0 + ph.slots - ph.window + RING
                split_to(min(base + RING + 1, free))
                for fn in late:
                    fn()
                split_to(free)
                if read:
                    read(0)
                split_to(base + ph.slots + 4)
                if b is not None:
                    x_part(b, 0)
                if read:
                    read(1)

            def copy_rows(ph, m, dst, func=ACT.Copy, sign=None, scaled=True):
                act.wait_ge(sums_done, ph.group0 + m + 1)
                kw = dict(scale=r_in[:, m % 2:m % 2 + 1]) if scaled else {}
                act.activation(dst, sums[(ph.group0 + m) % BANKS][:, :], func, **kw).then_inc(act_read, 1)

            def start(ph, b):
                split_to(ph.slot0 + 6)
                x_part(b, 1)
                split_to(ph.slot0 + 8)

            def ffn(f, b):
                ph = PHASES[f"ffn_in{f}"]

                def silu(m, j=None):
                    act.wait_ge(sums_done, lin(ph.group0 + m + 1, 4, j))
                    if m >= 2:
                        act.wait_ge(dve_read, lin(ph.dve0 + m - 1, 4, j))
                    t = m % 2
                    act.activation(work[:, t * FB:(t + 1) * FB], sums[(ph.group0 + m) % BANKS][:, 0:FB], ACT.Silu,
                                   scale=r_in[:, t:t + 1]).then_inc(act_read, 1)

                def hidden_hi(i, j=None):
                    act.wait_ge(hid_turned, lin(f * FI + i + 1, 2, j))
                    at = lin(2 * i, 4, j)
                    act.activation(y_hi[:, bass.ds(at, 2), :] if j is not None else y_hi[:, at:at + 2, :],
                                   turn[0][:, :].rearrange("p (c t) -> p c t", c=2), ACT.Copy).then_inc(y_hi_made, 1)

                start(ph, b)
                for t in range(NT):
                    act.wait_ge(r_in_made, 2 * b + t + 1)
                    silu(t)
                with act.Fori(0, (FI - 1) // 2) as j:
                    for s in range(2):
                        for k in range(4):
                            split(ph.slot0 + 8 + 4 * s + k, j)
                        silu(2 + 2 * s, j)
                        hidden_hi(s, j)
                        silu(3 + 2 * s, j)
                split_next[0] = ph.slot0 + 4 * FI + 4

                def late():
                    hidden_hi(FI - 1)
                    if f == 0:
                        for k in range(2):
                            act.wait_ge(angle_made, k + 1)
                            act.activation(trig[:, k].rearrange("p t n -> p (t n)"),
                                           work[:, (AW_K, AW_ANGLE)[k]:(AW_K, AW_ANGLE)[k] + 2 * P], ACT.Sin).then_inc(trig_made, 1)
                    if f % 2:
                        act.wait_ge(p_turned, f // 2 + 1)
                        act.activation(p_hi[:, :, :], turn[1][:, :].rearrange("p (c t) -> p c t", c=2),
                                       ACT.Copy).then_inc(p_hi_made, 1)

                out_phase(f"down{f}", b + 1, [late], lambda t: squares(f"down{f}", t))

            act.wait_ge(const_made, 1)
            act.activation(stat[:, 135:136], neg_half[:, 0:1], ACT.Copy).then_inc(act_read, BANKS)
            x_part(0, 0)
            ffn(0, 0)

            ph = PHASES["ret_in"]
            b = 1
            start(ph, b)

            def ret_y_hi(hd):
                for i in range(2):
                    act.wait_ge(mx["turned"], ret_turned(hd, i, True))
                    act.activation(y_hi[:, 4 * hd + 2 * i:4 * hd + 2 * i + 2, :],
                                   turn[i][:, :].rearrange("p (c t) -> p c t", c=2), ACT.Copy).then_inc(y_hi_made, 1)

            for hd in range(RH):
                m = 6 * hd
                for t in range(NT):
                    if hd == 0:
                        act.wait_ge(r_in_made, 2 * b + t + 1)
                    else:
                        act.wait_ge(mx["roped"], 2 * (hd - 1) + t + 1)
                    dst = work[:, RW_QK + t * 512:RW_QK + (t + 1) * 512]
                    copy_rows(ph, m + t, dst)
                    if t == 0 and hd:
                        ret_y_hi(hd - 1)
                split_to(ph.slot0 + 12 * hd + 12)
                for t in range(NT):
                    if hd:
                        act.wait_ge(mx["mixed"], 2 * hd)
                    copy_rows(ph, m + 2 + t, work[:, RW_V + t * 512:RW_V + (t + 1) * 512])
                    if t == 0:
                        for i in range(2):
                            act.wait_ge(mx["turned"], ret_turned(hd, i))
                            if hd:
                                act.wait_ge(mx["scores"], hd)
                            act.activation(work[:, RW_QKT + 512 * i:RW_QKT + 512 * (i + 1)], turn[i][:, :],
                                           ACT.Copy).then_inc(mx["flat"], 1)
                split_to(ph.slot0 + 12 * hd + 16)
                for t in range(NT):
                    if hd:
                        act.wait_ge(mx["y"], 2 * (hd - 1) + t + 1)
                    copy_rows(ph, m + 4 + t, work[:, RW_G + t * 512:RW_G + (t + 1) * 512], ACT.Silu)
                split_to(ph.slot0 + 12 * hd + 20) if hd < RH - 1 else None
            out_phase("ret_out", 2, [lambda: ret_y_hi(RH - 1)], lambda t: squares("ret_out", t))

            def ple(layer, b):
                ph = PHASES[f"ple_proj{layer}"]
                gate = PHASES[f"ple_gate{layer}"]
                split_to(ph.slot0 + 6)
                for m in range(4):
                    if m == 3:
                        x_part(b, 1)
                    copy_rows(ph, m, work[:, EW_E + (2 * (m % 2) + m // 2) * 512:EW_E + (2 * (m % 2) + m // 2 + 1) * 512],
                              scaled=False)
                split_to(ph.slot0 + 8)
                for t in range(NT):
                    act.wait_ge(r_in_made, 2 * b + t + 1)

                def read(t):
                    for n in range(2):
                        g = 2 * t + n
                        act.wait_ge(sums_done, gate.group0 + g + 1)
                        act.activation(work[:, EW_S + g * 512:EW_S + (g + 1) * 512],
                                       sums[(gate.group0 + g) % BANKS][:, :], ACT.Sigmoid,
                                       scale=r_in[:, t:t + 1]).then_inc(act_read, 1)
                    for n in range(2):
                        g = 2 * t + n
                        act.wait_ge(gated, 4 * layer + g + 1)
                        squared(gated_sq, 4 * layer + g + 1)
                        act.activation(junk[:, 0:COLS], work[:, EW_S + g * 512:EW_S + (g + 1) * 512], ACT.Square,
                                       accum_out=f_sq[:, g:g + 1]).then_inc(gated_sq, 1)

                out_phase(f"ple_gate{layer}", b + 1, [], read)

            ffn(1, 2)
            ple(0, 3)
            ffn(2, 4)

            ph = PHASES["sb_in"]
            b = 5
            start(ph, b)
            for t in range(NT):
                act.wait_ge(r_in_made, 2 * b + t + 1)

            def sb_rows(m):
                half, which, t = m // 6, (m % 6) // 2, m % 2
                if which < 2 and m >= 2:
                    act.wait_ge(sbs["turned"], 4 * half + 2 * which)
                if which == 2 and half:
                    act.wait_ge(sbs["o"], 4)
                at = (SW_QK if which < 2 else SW_V) + t * 512
                act.wait_ge(sums_done, ph_sb.group0 + m + 1)
                act.activation(work[:, at:at + 512], sums[(ph_sb.group0 + m) % BANKS][:, :], ACT.Copy,
                               scale=r_in[:, t:t + 1]).then_inc(act_read, 1)

            ph_sb = ph

            def sb_flat(which, half):
                for i in range(2):
                    act.wait_ge(sbs["turned"], 4 * half + 2 * which + i + 1)
                    if half:
                        act.wait_ge(sbs["z"], 4)
                    at = (SW_QT if which == 0 else SW_KT) + 512 * i
                    act.activation(work[:, at:at + 512], turn[2 * which + i][:, :], ACT.Copy,
                                   scale=(SDH ** -0.5 if which == 0 else 1.0)).then_inc(sbs["flat"], 1)

            def sb_log(hd):
                k = hd % 4
                at = work[:, SW_HEAD + k * 768:SW_HEAD + k * 768 + 384]
                act.wait_ge(sbs["z"], hd + 1)
                act.activation(at, turn[k][:, 0:384], ACT.Abs).then_inc(sbs["act_step"], 1)
                act.wait_ge(sbs["act_step"], 2 * hd + 1)
                act.activation(at, at, ACT.Exp, scale=-1.0).then_inc(sbs["act_step"], 1)
                act.wait_ge(sbs["act_step"], 2 * hd + 2)
                act.activation(at, at, ACT.Ln, bias=1.0).then_inc(sbs["log"], 1)

            def sb_exp(hd):
                k = hd % 4
                act.wait_ge(sbs["rem"], hd + 1)
                act.activation(work[:, SW_HEAD + k * 768:SW_HEAD + k * 768 + 384], turn[k][:, 0:384],
                               ACT.Exp).then_inc(sbs["a"], 1)

            def sb_y_hi(hd):
                act.wait_ge(sbs["o"], hd + 1)
                act.activation(y_hi[:, hd, :], turn[hd % 4][:, 0:SEQ], ACT.Copy).then_inc(y_hi_made, 1)

            s0 = ph.slot0
            sb_rows(0); sb_rows(1)
            split_to(s0 + 12)
            sb_rows(2); sb_flat(0, 0); sb_rows(3)
            split_to(s0 + 16)
            sb_rows(4); sb_flat(1, 0); sb_rows(5)
            act.preload_act_table_set("natural_log_exp_and_others")
            for hd in range(2):
                sb_log(hd)
            split_to(s0 + 20)
            for hd in range(2, 4):
                sb_log(hd)
            sb_rows(6)
            sb_exp(0); sb_exp(1)
            sb_rows(7)
            split_to(s0 + 24)
            sb_exp(2); sb_exp(3)
            sb_y_hi(0); sb_y_hi(1)
            sb_rows(8)
            sb_y_hi(2); sb_y_hi(3)
            sb_flat(0, 1)
            sb_rows(9); sb_flat(1, 1)
            split_to(s0 + 28)
            sb_rows(10)
            sb_log(4); sb_log(5)
            sb_rows(11)
            sb_log(6); sb_log(7)
            split_to(s0 + 32)

            def sb_late():
                for hd in range(4, 8):
                    sb_exp(hd)
                for hd in range(4, 8):
                    sb_y_hi(hd)

            out_phase("sb_out", 6, [sb_late], lambda t: squares("sb_out", t))

            ffn(3, 6)
            ple(1, 7)

            ph = PHASES["conv_in"]
            b = 8
            start(ph, b)
            for t in range(NT):
                act.wait_ge(r_in_made, 2 * b + t + 1)

            def cv_y_hi(half):
                for c in range(4):
                    act.wait_ge(cv["y"], 4 * half + c + 1)
                    act.activation(y_hi[:, 4 * half + c, :], work[:, CW_Y + c * SEQ:CW_Y + (c + 1) * SEQ],
                                   ACT.Copy).then_inc(y_hi_made, 1)

            for m in range(16):
                half, i, t = m // 8, (m % 8) // 2, m % 2
                if half and t == 0:
                    act.wait_ge(cv["turned"], 2 if i < 2 else 4)
                at = (CW_C, CW_X, CW_B, CW_Z)[i] + t * 512
                copy_rows(ph, m, work[:, at:at + 512], ACT.Silu if i == 3 else ACT.Copy)
                if m in (5, 13):
                    for k in range(2):
                        act.wait_ge(cv["turned"], 4 * half + k + 1)
                        if half:
                            act.wait_ge(cv["step"], 12)
                        else:
                            act.wait_ge(cv["pad"], 1)
                        act.activation(work[:, CW_U:CW_U + 4 * UPAD].rearrange("p (c t) -> p c t", c=4)[:, 2 * k:2 * k + 2, 2:UPAD],
                                       turn[k][:, :].rearrange("p (c t) -> p c t", c=2), ACT.Copy).then_inc(cv["flat"], 1)
                if m == 10:
                    cv_y_hi(0)
                if m % 2 == 1:
                    split_to(min(ph.slot0 + 4 * (m // 2) + 12, ph.slot0 + 36))
            out_phase("conv_out", 9, [lambda: cv_y_hi(1)], None)

            ph = PHASES["moba_in"]
            b = 9
            start(ph, b)
            for t in range(NT):
                act.wait_ge(r_in_made, 2 * b + t + 1)

            def mb_flat(which, half):
                for i in range(2):
                    act.wait_ge(mb["turned"], 4 * half + 2 * which + i + 1)
                    act.activation(mb_transposed(half)[which][:, 512 * i:512 * (i + 1)], turn[2 * which + i][:, :], ACT.Copy,
                                   scale=gains_b[:, 40 + which:41 + which]).then_inc(mb["flat"], 1)

            def mb_stage(k):
                for hd in range(2 * k - 2, 2 * k) if 1 <= k < MH // 2 + 1 else ():
                    at = MW_HEAD + (hd % 2) * 768
                    act.wait_ge(mb["pt"], hd + 1)
                    if hd >= 2:
                        act.wait_ge(mb["o"], hd - 1)
                    act.activation(work[:, at + 384:at + 768], turn[2][:, 0:384], ACT.Copy).then_inc(mb["pt_flat"], 1)
                for hd in range(2 * k, 2 * k + 2) if k < MH // 2 else ():
                    sm = soft[:, 6 * (hd % 8):6 * (hd % 8) + 6]
                    at = MW_HEAD + (hd % 2) * 768
                    act.wait_ge(mb["max"], 2 * hd + 2)
                    act.activation(sm[:, 0:2], sm[:, 0:2], ACT.Copy, scale=-(MDH ** -0.5)).then_inc(mb["negmax"], 1)
                    act.wait_ge(mb["negmax"], hd + 1)
                    for t in range(NT):
                        cols = slice(at, at + P) if t == 0 else slice(at + P, at + 384)
                        act.activation(work[:, cols], work[:, cols], ACT.Exp, scale=MDH ** -0.5, bias=sm[:, t:t + 1],
                                       accum_out=sm[:, 2 + t:3 + t]).then_inc(mb["exp"], 1)

            def mb_y_hi(half, i):
                act.wait_ge(mb["y_turned"], 2 * half + i + 1)
                act.activation(y_hi[:, 4 * half + 2 * i:4 * half + 2 * i + 2, :],
                               mb_y_bank(half, i)[:, :].rearrange("p (c t) -> p c t", c=2), ACT.Copy).then_inc(y_hi_made, 1)

            for m in range(16):
                (i, half), t = MOBA_BLOCKS[m // 2], m % 2
                if i < 2:
                    if half:
                        act.wait_ge(mb["turned"], 2 * i + 2)
                    dst = work[:, (MW_Q, MW_K)[i] + t * 512:(MW_Q, MW_K)[i] + (t + 1) * 512]
                elif i == 2:
                    dst = mb_values(half)[:, t, :]
                else:
                    if half:
                        act.wait_ge(mb["gated"], t + 1)
                    dst = work[:, MW_Z + t * 512:MW_Z + (t + 1) * 512]
                copy_rows(ph, m, dst, ACT.Silu if i == 3 else ACT.Copy)
                if m in (1, 3, 5):
                    split_to(ph.slot0 + 2 * m + 10)
                if m in (3, 5, 7, 9):
                    mb_flat(*{3: (0, 0), 5: (1, 0), 7: (0, 1), 9: (1, 1)}[m])
                if m == 9:
                    split_to(ph.slot0 + 24)
                if m >= 8:
                    mb_stage(m - 8)
                    split_to(min(ph.slot0 + 24 + 2 * (m - 8), SLOTS - 4) if m > 8 else ph.slot0 + 22)
                if m >= 14:
                    mb_y_hi(0, m - 14)
            mb_stage(8)
            split_to(SLOTS - 2)
            mb_stage(9)
            split_to(SLOTS)
            mb_y_hi(1, 0)
            mb_y_hi(1, 1)

        @block.vector
        def _(dve):
            split_next = [0]

            def split(n, j=None):
                dve.wait_ge(hi_made, lin(n + 1, RING, j))
                dve.tensor_tensor(w_lo[:, n % RING].rearrange("p c n -> p (c n)"),
                                  raw[:, n % RAW].rearrange("p c n -> p (c n)"),
                                  w_hi[:, n % RING].rearrange("p c n -> p (c n)").bitcast(F32), ALU.subtract).then_inc(lo_made, 1)

            def split_to(n):
                while split_next[0] < min(n, SLOTS):
                    split(split_next[0])
                    split_next[0] += 1

            def x_part(b, t):
                gain = pre_gain[boundaries[b]]
                for q in range(2):
                    dve.wait_ge(h_turned, 4 * b + 2 * t + q + 1)
                    dve.tensor_tensor(xg[:, q, :].rearrange("p (c t) -> p c t", c=4),
                                      turn[2 * t + q][:, :].rearrange("p (c t) -> p c t", c=4),
                                      gain[:, 4 * q:4 * q + 4].unsqueeze(2).to_broadcast([P, 4, P]), ALU.mult).then_inc(xg_made, 1)
                for q in range(2):
                    dve.wait_ge(x_hi_made, 4 * b + 2 * t + q + 1)
                    dve.tensor_tensor(x_lo[:, 4 * q:4 * q + 4, t * P:(t + 1) * P],
                                      xg[:, q, :].rearrange("p (c t) -> p c t", c=4),
                                      x_hi[:, 4 * q:4 * q + 4, t * P:(t + 1) * P].bitcast(F32), ALU.subtract).then_inc(x_lo_made, 1)

            def gain_rows(name, t):
                ph = PHASES[name]
                dve.wait_ge(post_loaded, 16 * (post_order.index(name) + 1))
                for n in range(2):
                    dve.wait_ge(act_read, ph.act0 + 2 * t + n + 1)
                    dve.tensor_tensor(fg[:, t, n, :], sums[(ph.group0 + 2 * t + n) % BANKS][:, :],
                                      post_gain[:, n * COLS:(n + 1) * COLS], ALU.mult).then_inc(dve_read, 1)

            def add_normed(name, b, t, ready):
                ready()
                dve.wait_ge(r_post_made, 2 * post_order.index(name) + t + 1)
                for q in range(2):
                    dve.scalar_tensor_tensor(out=h[:, t, q * COLS:(q + 1) * COLS], in0=fg[:, t, q, :],
                                             scalar=r_post[:, t:t + 1], in1=h[:, t, q * COLS:(q + 1) * COLS],
                                             op0=ALU.mult, op1=ALU.add).then_inc(h_new, 1)

            def out_phase(name, b, late, first, then):
                ph = PHASES[name]
                base, free = ph.slot0, ph.slot0 + ph.slots - ph.window + RING
                split_to(min(base + RING + 1, free))
                for fn in late:
                    fn()
                split_to(free)
                first(0)
                then(0)
                split_to(base + ph.slots + 4)
                if b is not None:
                    x_part(b, 0)
                first(1)
                then(1)

            def plain_post(name, b, late):
                ph = PHASES[name]
                out_phase(name, b, late, lambda t: gain_rows(name, t),
                          lambda t: add_normed(name, b, t, lambda: dve.wait_ge(dve_read, ph.dve0 + 2 * t + 2)))

            def start(ph, b):
                x_part(b, 1)
                split_to(ph.slot0 + 8)

            def ffn(f, b):
                ph = PHASES[f"ffn_in{f}"]

                def hidden(m, j=None):
                    t = m % 2
                    dve.wait_ge(act_read, lin(ph.act0 + m + 1, 4, j))
                    if m >= 2:
                        dve.wait_ge(hid_turned, lin(f * FI + m // 2, 2, j))
                    dve.scalar_tensor_tensor(out=work[:, HW_HID + t * FB:HW_HID + (t + 1) * FB],
                                             in0=sums[(ph.group0 + m) % BANKS][:, FB:2 * FB], scalar=r_in[:, t:t + 1],
                                             in1=work[:, HW_SILU + t * FB:HW_SILU + (t + 1) * FB],
                                             op0=ALU.mult, op1=ALU.mult)\
                       .then_inc(dve_read, 1)

                def hidden_lo(i, j=None):
                    dve.wait_ge(y_hi_made, lin(y_base(f"ffn{f}") + i + 1, 2, j))
                    at = slice(2 * i, 2 * i + 2) if j is None else bass.ds(lin(2 * i, 4, j), 2)
                    dve.tensor_tensor(y_lo[:, at, :], turn[0][:, :].rearrange("p (c t) -> p c t", c=2),
                                      y_hi[:, at, :].bitcast(F32), ALU.subtract).then_inc(y_lo_made, 1)

                start(ph, b)
                hidden(0)
                hidden(1)
                with dve.Fori(0, (FI - 1) // 2) as j:
                    for s in range(2):
                        for k in range(4):
                            split(ph.slot0 + 8 + 4 * s + k, j)
                        hidden(2 + 2 * s, j)
                        hidden_lo(s, j)
                        hidden(3 + 2 * s, j)
                split_next[0] = ph.slot0 + 4 * FI + 4

                def late():
                    hidden_lo(FI - 1)
                    if f == 0:
                        angles()
                    if f % 2:
                        dve.wait_ge(p_hi_made, f // 2 + 1)
                        dve.tensor_tensor(p_lo[:, :, :], turn[1][:, :].rearrange("p (c t) -> p c t", c=2),
                                          p_hi[:, :, :].bitcast(F32), ALU.subtract).then_inc(p_lo_made, 1)

                plain_post(f"down{f}", b + 1, [late])

            def angles():
                dve.wait_ge(rope_loaded, 16 * 3)
                steps = [0]

                def step(ins):
                    steps[0] += 1
                    ins.then_inc(trig_step, 1)
                    dve.wait_ge(trig_step, steps[0])

                A = work[:, AW_ANGLE:AW_ANGLE + 2 * P]
                K = work[:, AW_K:AW_K + 2 * P]
                KH = work[:, AW_KH:AW_KH + 2 * P]
                step(dve.tensor_copy(pos_f, work[:, AW_POS:AW_POS + 2].bitcast(I32)))
                for t in range(NT):
                    step(dve.tensor_scalar(work[:, AW_ANGLE + t * P:AW_ANGLE + (t + 1) * P], work[:, AW_FREQ:AW_FREQ + P],
                                           pos_f[:, t:t + 1], None, ALU.mult))
                step(dve.tensor_scalar(K, A, 1.0 / TWO_PI, MAGIC, ALU.mult, ALU.add))
                step(dve.tensor_scalar(K, K, -MAGIC, None, ALU.add))
                step(dve.tensor_scalar(KH, K, 2048.0 * MAGIC, None, ALU.add))
                step(dve.tensor_scalar(KH, KH, -2048.0 * MAGIC, None, ALU.add))
                step(dve.tensor_tensor(K, K, KH, ALU.subtract))
                for part in two_pi_parts():
                    for k in (KH, K):
                        step(dve.scalar_tensor_tensor(out=A, in0=k, scalar=-part, in1=A, op0=ALU.mult, op1=ALU.add))
                step(dve.tensor_scalar(A, A, 3.1415925, -3.1415925, ALU.min, ALU.max))
                step(dve.tensor_scalar(K, A, -1.0, None, ALU.mult))
                step(dve.tensor_tensor(K, K, A, ALU.max))
                dve.tensor_scalar(K, K, -1.0, float(np.pi / 2), ALU.mult, ALU.add).then_inc(angle_made, 2)

            dve.wait_ge(const_made, 1)
            dve.tensor_copy(stat[:, 134:135], neg_half[:, 0:1]).then_inc(dve_read, BANKS)
            dve.wait_ge(gains_turned, 1)
            dve.tensor_copy(gains_a[:, :], turn[2][:, 0:P])
            dve.tensor_copy(gains_b[:, :], turn[2][:, P:P + 42]).then_inc(gains_made, 1)
            dve.wait_ge(gains_made, 1)
            x_part(0, 0)
            split_to(4)
            ffn(0, 0)

            ph = PHASES["ret_in"]
            start(ph, 1)
            counts = {"rope": 0, "gn": 0, "y": 0}

            def rope(hd, t):
                rows = work[:, RW_QK + t * 512:RW_QK + (t + 1) * 512].rearrange("p (x n) -> p x n", x=4)
                dst = work[:, RW_QKR + t * 512:RW_QKR + (t + 1) * 512].rearrange("p (i e n) -> p i e n", i=2, e=2)
                C = work[:, RW_ROPE:RW_ROPE + 512].rearrange("p (x n) -> p x n", x=4)
                S = work[:, RW_ROPE + 512:RW_ROPE + 1024].rearrange("p (x n) -> p x n", x=4)
                C4, S4 = (work[:, RW_ROPE + o:RW_ROPE + o + 512].rearrange("p (i e n) -> p i e n", i=2, e=2) for o in (0, 512))
                dve.wait_ge(act_read, ph.act0 + 6 * hd + t + 1)
                if 2 * hd + t:
                    dve.wait_ge(mx["roped"], 2 * hd + t)
                dve.tensor_tensor(C, rows, trig[:, 0, t, :].unsqueeze(1).to_broadcast([P, 4, P]), ALU.mult).then_inc(mx["rope_step"], 1)
                dve.tensor_tensor(S, rows, trig[:, 1, t, :].unsqueeze(1).to_broadcast([P, 4, P]), ALU.mult).then_inc(mx["rope_step"], 1)
                counts["rope"] += 2
                dve.wait_ge(mx["rope_step"], counts["rope"])
                if hd:
                    dve.wait_ge(mx["turned"], ret_turned(hd - 1, 1))
                dve.tensor_tensor(dst[:, :, 0, :], C4[:, :, 0, :], S4[:, :, 1, :], ALU.subtract)
                dve.tensor_tensor(dst[:, :, 1, :], C4[:, :, 1, :], S4[:, :, 0, :], ALU.add).then_inc(mx["roped"], 1)

            def weights(hd):
                dve.wait_ge(decay_loaded, 16 * (hd + 1))
                dve.wait_ge(mx["scores"], hd + 1)
                if hd:
                    dve.wait_ge(mx["mixed"], 2 * hd)
                dve.tensor_tensor(work[:, RW_P:RW_P + SEQ], turn[2][:, 0:SEQ], work[:, RW_DECAY:RW_DECAY + SEQ],
                                  ALU.mult).then_inc(mx["weights"], 1)
                dve.tensor_tensor(work[:, RW_P + SEQ:RW_P + 384], turn[2][:, SEQ:384], work[:, RW_DECAY:RW_DECAY + P],
                                  ALU.mult).then_inc(mx["weights"], 1)

            def stats(hd):
                for t in range(NT):
                    dve.wait_ge(mx["mixed"], 2 * hd + t + 1)
                    dve.bn_stats(gn_stats[:, 6 * t:6 * t + 6], turn[3 - t][:, :]).then_inc(mx["gn_step"], 1)
                    counts["gn"] += 1
                    dve.wait_ge(mx["gn_step"], counts["gn"])
                    dve.bn_aggr(gn_mv[:, 2 * t:2 * t + 2], gn_stats[:, 6 * t:6 * t + 6]).then_inc(mx["stats"], 1)

            def gate(hd, t):
                g = work[:, RW_G + t * 512:RW_G + (t + 1) * 512]
                dve.wait_ge(gn_loaded, 16 * (hd + 1))
                dve.wait_ge(act_read, ph.act0 + 6 * hd + 4 + t + 1)
                dve.tensor_tensor(g, g, work[:, RW_GN:RW_GN + 512], ALU.mult).then_inc(mx["gate"], 1)

            def rows(hd, t):
                y = work[:, RW_Y + t * 512:RW_Y + (t + 1) * 512]
                dve.wait_ge(mx["gn_r"], 2 * hd + t + 1)
                if hd:
                    dve.wait_ge(mx["turned"], ret_turned(hd - 1, 1, True))
                dve.tensor_scalar(y, turn[3 - t][:, :], gn_mv[:, 2 * t:2 * t + 1], gn_r[:, t:t + 1],
                                  ALU.subtract, ALU.mult).then_inc(mx["y_step"], 1)
                counts["y"] += 1
                dve.wait_ge(mx["y_step"], counts["y"])
                dve.wait_ge(mx["gate"], 2 * hd + t + 1)
                dve.tensor_tensor(y, y, work[:, RW_G + t * 512:RW_G + (t + 1) * 512], ALU.mult).then_inc(mx["y"], 1)

            def y_lo_of(bank, base, k, width=2):
                dve.wait_ge(y_hi_made, base)
                dve.tensor_tensor(y_lo[:, k:k + width, :], bank.rearrange("p (c t) -> p c t", c=width),
                                  y_hi[:, k:k + width, :].bitcast(F32), ALU.subtract).then_inc(y_lo_made, 1)

            def ret_y_lo(hd):
                for i in range(2):
                    y_lo_of(turn[i][:, :], y_base("ret") + 2 * hd + i + 1, 4 * hd + 2 * i)

            for hd in range(RH):
                if hd == 0:
                    dve.wait_ge(trig_made, 2)
                rope(hd, 0)
                if hd:
                    ret_y_lo(hd - 1)
                rope(hd, 1)
                split_to(ph.slot0 + 12 * hd + 12)
                weights(hd)
                split_to(ph.slot0 + 12 * hd + 16)
                stats(hd)
                for t in range(NT):
                    gate(hd, t)
                    rows(hd, t)
                if hd < RH - 1:
                    split_to(ph.slot0 + 12 * hd + 20)
            plain_post("ret_out", 2, [lambda: ret_y_lo(RH - 1)])

            def ple(layer, b):
                ph = PHASES[f"ple_proj{layer}"]
                name = f"ple_gate{layer}"
                split_to(ph.slot0 + 6)
                x_part(b, 1)
                split_to(ph.slot0 + 8)

                def first(t):
                    for n in range(2):
                        g = 2 * t + n
                        s = work[:, EW_S + g * 512:EW_S + (g + 1) * 512]
                        dve.wait_ge(act_read, PHASES[name].act0 + g + 1)
                        dve.tensor_tensor(s, s, work[:, EW_E + g * 512:EW_E + (g + 1) * 512], ALU.mult).then_inc(gated, 1)
                    dve.wait_ge(post_loaded, 16 * (post_order.index(name) + 1))
                    for n in range(2):
                        g = 2 * t + n
                        dve.wait_ge(gated, 4 * layer + g + 1)
                        dve.tensor_tensor(fg[:, t, n, :], work[:, EW_S + g * 512:EW_S + (g + 1) * 512],
                                          post_gain[:, n * COLS:(n + 1) * COLS], ALU.mult).then_inc(fg_made, 1)

                out_phase(name, b + 1, [], first,
                          lambda t: add_normed(name, b + 1, t, lambda: dve.wait_ge(fg_made, 4 * layer + 2 * t + 2)))

            ffn(1, 2)
            ple(0, 3)
            ffn(2, 4)

            ph = PHASES["sb_in"]
            start(ph, 5)
            s0 = ph.slot0

            def sb_loss(hd):
                k = hd % 4
                at = SW_HEAD + k * 768
                dve.wait_ge(sbs["log"], hd + 1)
                dve.scalar_tensor_tensor(out=work[:, at + 384:at + 768], in0=turn[k][:, 0:384], scalar=0.0,
                                         in1=work[:, at:at + 384], op0=ALU.max, op1=ALU.add).then_inc(sbs["dve_step"], 1)
                dve.wait_ge(sbs["dve_step"], hd + 1)
                dve.wait_ge(mask_loaded, 16)
                dve.tensor_tensor(work[:, at + 384:at + 768], work[:, at + 384:at + 768], work[:, SW_MASK:SW_MASK + 384],
                                  ALU.mult).then_inc(sbs["loss"], 1)

            def sb_y_lo(hd):
                y_lo_of(turn[hd % 4][:, 0:SEQ], y_base("sb") + hd + 1, hd, 1)

            split_to(s0 + 16)
            sb_loss(0); sb_loss(1)
            split_to(s0 + 20)
            sb_loss(2); sb_loss(3)
            split_to(s0 + 24)
            for hd in range(4):
                sb_y_lo(hd)
            split_to(s0 + 28)
            for hd in range(4, 8):
                sb_loss(hd)
            split_to(s0 + 32)

            plain_post("sb_out", 6, [lambda: [sb_y_lo(hd) for hd in range(4, 8)]])

            ffn(3, 6)
            ple(1, 7)

            ph = PHASES["conv_in"]
            dve.memset(work[:, CW_U:CW_U + 4 * UPAD].rearrange("p (c t) -> p c t", c=4)[:, :, 0:2], 0.0).then_inc(cv["pad"], 1)
            start(ph, 8)

            def cv_mul(half, which, t):
                a, b = ((CW_C, CW_X), (CW_B, CW_Z))[which]
                dve.wait_ge(act_read, ph.act0 + 8 * half + 4 * which + 2 + t + 1)
                dve.tensor_tensor(work[:, a + t * 512:a + (t + 1) * 512], work[:, a + t * 512:a + (t + 1) * 512],
                                  work[:, b + t * 512:b + (t + 1) * 512], ALU.mult).then_inc(cv["mul"], 1)

            def cv_conv(half):
                for k in range(3):
                    for c in range(4):
                        u = work[:, CW_U + c * UPAD + k:CW_U + c * UPAD + k + SEQ]
                        y = work[:, CW_Y + c * SEQ:CW_Y + (c + 1) * SEQ]
                        tap = gains_b[:, 16 + 8 * k + 4 * half + c:17 + 8 * k + 4 * half + c]
                        if k == 0:
                            dve.wait_ge(cv["flat"], 2 * half + c // 2 + 1)
                            if half:
                                dve.wait_ge(y_lo_made, y_base("conv") + 4)
                            dve.tensor_scalar(y, u, tap, None, ALU.mult).then_inc(cv["step"], 1)
                        else:
                            dve.wait_ge(cv["step"], 12 * half + 4 * (k - 1) + c + 1)
                            dve.scalar_tensor_tensor(out=y, in0=u, scalar=tap, in1=y, op0=ALU.mult,
                                                     op1=ALU.add).then_inc(cv["step"], 1)

            def cv_gate(half):
                for c in range(4):
                    y = work[:, CW_Y + c * SEQ:CW_Y + (c + 1) * SEQ]
                    dve.wait_ge(cv["step"], 12 * half + 8 + c + 1)
                    dve.wait_ge(cv["turned"], 4 * half + 2 + c // 2 + 1)
                    dve.tensor_tensor(y, y, turn[2 + c // 2][:, (c % 2) * SEQ:(c % 2 + 1) * SEQ], ALU.mult).then_inc(cv["y"], 1)
                for c in range(4):
                    y_lo_of(work[:, CW_Y + c * SEQ:CW_Y + (c + 1) * SEQ], y_base("conv") + 4 * half + c + 1, 4 * half + c, 1)

            split_to(ph.slot0 + 14)
            cv_mul(0, 0, 0); cv_mul(0, 0, 1)
            split_to(ph.slot0 + 20)
            cv_conv(0)
            cv_mul(0, 1, 0); cv_mul(0, 1, 1)
            split_to(ph.slot0 + 24)
            cv_gate(0)
            split_to(ph.slot0 + 30)
            cv_mul(1, 0, 0); cv_mul(1, 0, 1)
            split_to(ph.slot0 + 36)
            cv_conv(1)
            cv_mul(1, 1, 0); cv_mul(1, 1, 1)

            def add_sums(name):
                ph = PHASES[name]

                def then(t):
                    for n in range(2):
                        dve.wait_ge(sums_done, ph.group0 + 2 * t + n + 1)
                        cols = slice(n * COLS, (n + 1) * COLS)
                        dve.tensor_tensor(h[:, t, cols], sums[(ph.group0 + 2 * t + n) % BANKS][:, :], h[:, t, cols],
                                          ALU.add).then_inc(h_new, 1)
                return then

            out_phase("conv_out", 9, [lambda: cv_gate(1)], lambda t: None, add_sums("conv_out"))

            ph = PHASES["moba_in"]
            start(ph, 9)
            mb_steps = [0]

            def mb_norm(which, half):
                k = 2 * half + which
                at = (MW_Q, MW_K)[which]
                for t in range(NT):
                    rows = work[:, at + t * 512:at + (t + 1) * 512]
                    sq = work[:, MW_SQ:MW_SQ + 512]
                    dve.wait_ge(act_read, ph.act0 + 4 * half + 2 * which + t + 1)
                    if 2 * k + t:
                        dve.wait_ge(mb["sq"], 2 * k + t)
                    dve.tensor_tensor(sq, rows, rows, ALU.mult).then_inc(mb["sq_step"], 1)
                    mb_steps[0] += 1
                    dve.wait_ge(mb["sq_step"], mb_steps[0])
                    dve.tensor_reduce(qk_sq[:, 8 * t:8 * t + 8], sq.rearrange("p (h d) -> p h d", h=8), AX_X, ALU.add).then_inc(mb["sq"], 1)
                for t in range(NT):
                    rows = work[:, at + t * 512:at + (t + 1) * 512].rearrange("p (h d) -> p h d", h=8)
                    dve.wait_ge(mb["r"], k + 1)
                    dve.tensor_tensor(rows, rows, qk_r[:, 8 * t:8 * t + 8].unsqueeze(2).to_broadcast([P, 8, MDH]),
                                      ALU.mult).then_inc(mb["normed"], 1)

            def mb_finish(hd):
                half = hd // 8
                sm = soft[:, 6 * (hd % 8):6 * (hd % 8) + 6]
                dve.wait_ge(mb["exp"], 2 * hd + 2)
                dve.reciprocal(sm[:, 4:6], sm[:, 2:4]).then_inc(mb["recip"], 1)
                dve.wait_ge(mb["turned"], 6 + 2 * half)
                dve.wait_ge(mb["recip"], hd + 1)
                dve.wait_ge(mb["o"], hd + 1)
                for t in range(NT):
                    at = (MW_Q, MW_K)[half] + t * 512 + (hd % 8) * MDH
                    dve.tensor_scalar(work[:, at:at + MDH], turn[hd % 2][:, 384 + t * MDH:384 + (t + 1) * MDH],
                                      sm[:, 4 + t:5 + t], None, ALU.mult).then_inc(mb["rows"], 1)

            def mb_gate(half):
                dve.wait_ge(mb["rows"], 16 * half + 16)
                for t in range(NT):
                    y = work[:, (MW_Q, MW_K)[half] + t * 512:(MW_Q, MW_K)[half] + (t + 1) * 512]
                    dve.wait_ge(act_read, ph.act0 + 12 + 2 * half + t + 1)
                    dve.tensor_tensor(y, y, work[:, MW_Z + t * 512:MW_Z + (t + 1) * 512], ALU.mult).then_inc(mb["gated"], 1)

            def mb_stage(k):
                for hd in range(2 * k - 4, 2 * k - 2) if k >= 2 else ():
                    mb_finish(hd)
                for hd in range(2 * k, 2 * k + 2) if k < MH // 2 else ():
                    sm = soft[:, 6 * (hd % 8):6 * (hd % 8) + 6]
                    at = MW_HEAD + (hd % 2) * 768
                    slope = float(np.float32(2.0 ** (-8.0 * (hd + 1) / MH)))
                    dve.wait_ge(mask_loaded, 32)
                    dve.wait_ge(mb["s"], hd + 1)
                    if hd >= 2:
                        dve.wait_ge(mb["pt"], hd - 1)
                    dve.scalar_tensor_tensor(out=work[:, at:at + 384], in0=work[:, MW_DIST:MW_DIST + 384],
                                             scalar=-slope * MDH ** 0.5, in1=turn[hd % 2][:, 0:384],
                                             op0=ALU.mult, op1=ALU.add).then_inc(mb["t"], 1)
                    dve.wait_ge(mb["t"], hd + 1)
                    dve.tensor_reduce(sm[:, 0:1], work[:, at:at + P], AX_X, ALU.max).then_inc(mb["max"], 1)
                    dve.tensor_reduce(sm[:, 1:2], work[:, at + P:at + 384], AX_X, ALU.max).then_inc(mb["max"], 1)

            def mb_y_lo(half, i):
                y_lo_of(mb_y_bank(half, i)[:, :], y_base("moba") + 2 * half + i + 1, 4 * half + 2 * i)

            s0 = ph.slot0
            mb_norm(0, 0)
            split_to(s0 + 12)
            mb_norm(1, 0)
            split_to(s0 + 16)
            mb_norm(0, 1)
            split_to(s0 + 20)
            mb_norm(1, 1)
            for k in range(8):
                mb_stage(k)
                if k == 5:
                    mb_gate(0)
                split_to(min(s0 + 24 + 2 * k, SLOTS - 4))
                if k >= 6:
                    mb_y_lo(0, k - 6)
            mb_stage(8)
            split_to(SLOTS - 2)
            mb_stage(9)
            mb_gate(1)
            split_to(SLOTS)
            mb_y_lo(1, 0)
            mb_y_lo(1, 1)
            then = add_sums("moba_out")
            then(0)
            then(1)


INPUTS = ["x", "p", "positions", "norm_gains", "ffn_w_gate", "ffn_w_up", "ffn_w_down", "ret_w_in", "ret_gn_gain",
          "ret_w_out", "sb_w_in", "sb_w_out", "ple_w_gate", "ple_w_proj", "norm_g_2", "conv_w_in_2", "conv_w_2",
          "conv_w_out_2", "attn_w_in_2", "q_norm_g_2", "k_norm_g_2", "attn_w_out_2"]


def kernel(**inputs):
    import concourse.bacc as bacc
    from concourse.bass_utils import run_bass_kernel_spmd

    nc = bacc.Bacc("TRN2", target_bir_lowering=False, num_devices=1)
    arrays, args = {}, []
    named = {name: np.ascontiguousarray(inputs[name]) for name in INPUTS}
    named["constants"] = constants()
    for name, a in named.items():
        arrays[f"in_{name}_dram"] = a
        args.append(nc.dram_tensor(f"in_{name}_dram", a.shape, mybir.dt.from_np(a.dtype), kind="ExternalInput").ap())
    out = nc.dram_tensor("out_0_dram", (1, SEQ, D), F32, kind="ExternalOutput").ap()
    build(nc, *args, out)
    r = run_bass_kernel_spmd(nc, [arrays], core_ids=[0])
    return r.results[0]["out_0_dram"]
```
